# Optimizing a Trainium2 kernel written in Bass

```python
import math
import jax
import jax.numpy as jnp
from jax import lax
import numpy as np

D_MODEL = 1024
BATCH = 1
SEQ = 512
DEPTH = 2

CTX_LEN = 256
GRID_W = 64
HEAD_DIM = 64
N_MIXERS = 4
GROUP_WIDTH = D_MODEL // N_MIXERS
GROUP_HEADS = GROUP_WIDTH // HEAD_DIM
Q_BLOCK = 128
MLA_NOPE = HEAD_DIM
MLA_ROPE = HEAD_DIM // 2
MLA_V = HEAD_DIM
MLA_KV_RANK = D_MODEL // 8
SWA_KV_HEADS = GROUP_HEADS // 2
SWA_WINDOW = 128
SWA_BLOCK = 128
NA_KH = 8
NA_KW = 16
NA_QB_W = 16
NA_KB_W = NA_QB_W + NA_KW
RET_CHUNK = 128
PEER_HEADS = 8
PEER_NKEYS = 128
PEER_EXPERTS = PEER_NKEYS * PEER_NKEYS
PEER_TOPK = 16
PEER_DKEY = 256
PEER_TOKEN_BLOCK = 128
ADA_CHUNKS = 6
ROPE_BASE = 10000.0
EPS = 1e-6
NEG_INF = -1e30

IN_SPLITS = (
    GROUP_HEADS * (MLA_NOPE + MLA_ROPE),
    MLA_KV_RANK,
    MLA_ROPE,
    GROUP_HEADS * HEAD_DIM,
    SWA_KV_HEADS * HEAD_DIM,
    SWA_KV_HEADS * HEAD_DIM,
    GROUP_WIDTH,
    GROUP_WIDTH,
    GROUP_WIDTH,
    GROUP_WIDTH,
    GROUP_WIDTH,
    GROUP_WIDTH,
    GROUP_WIDTH,
    GROUP_WIDTH,
)
IN_WIDTH = sum(IN_SPLITS)

kernel_name = "hybrid_parallel_heads_peer_flow_block"

def rmsnorm(x, g):
    xf = x.astype(jnp.float32)
    y = xf * lax.rsqrt(jnp.mean(xf * xf, axis=-1, keepdims=True) + EPS)
    return (y * g.astype(jnp.float32)).astype(x.dtype)

def modulate(h, shift, scale):
    return h * (1.0 + scale[:, None, :]) + shift[:, None, :]

def split_heads(t, n):
    b, s, _ = t.shape
    return t.reshape(b, s, n, -1).transpose(0, 2, 1, 3)

def merge_heads(t):
    b, n, s, d = t.shape
    return t.transpose(0, 2, 1, 3).reshape(b, s, n * d)

def softmax_f32(logits):
    return jax.nn.softmax(logits.astype(jnp.float32), axis=-1)

def axial_rope_tables(n_tok, rot_dim):
    quarter = rot_dim // 4
    inv = ROPE_BASE ** (-jnp.arange(quarter, dtype=jnp.float32) / quarter)
    t = jnp.arange(n_tok, dtype=jnp.int32)
    pos = jnp.stack([t // GRID_W, t % GRID_W], axis=-1).astype(jnp.float32)
    ang = pos[:, :, None] * inv
    return jnp.cos(ang), jnp.sin(ang)

def apply_axial_rope(x, cos, sin):
    shp = x.shape
    quarter = shp[-1] // 4
    xf = x.astype(jnp.float32).reshape(shp[:-1] + (2, 2, quarter))
    x1, x2 = xf[..., 0, :], xf[..., 1, :]
    out = jnp.stack([x1 * cos - x2 * sin, x1 * sin + x2 * cos], axis=-2)
    return out.reshape(shp).astype(x.dtype)

def dense_ctx_attention(q, k, v, scale, sink=None):
    s = jnp.einsum("bhqd,bhkd->bhqk", q, k).astype(jnp.float32) * scale
    if sink is not None:
        sink_col = jnp.broadcast_to(sink.astype(jnp.float32)[None, :, None, None], s.shape[:-1] + (1,))
        p = softmax_f32(jnp.concatenate([s, sink_col], axis=-1))[..., :-1]
    else:
        p = softmax_f32(s)
    return jnp.einsum("bhqk,bhkd->bhqd", p.astype(v.dtype), v)

def mla_kv(ckv, kv_norm_g, w_ukv):
    kv = split_heads(rmsnorm(ckv, kv_norm_g) @ w_ukv, GROUP_HEADS)
    return kv[..., :MLA_NOPE], kv[..., MLA_NOPE:]

def mla_mixer(q_l, ckv_l, kr_l, q_c, ckv_c, kr_c, kv_norm_g, w_ukv, cos, sin, with_ctx):
    h = GROUP_HEADS
    scale = (MLA_NOPE + MLA_ROPE) ** -0.5
    kn_l, v_l = mla_kv(ckv_l, kv_norm_g, w_ukv)
    kn_c, v_c = mla_kv(ckv_c, kv_norm_g, w_ukv)
    kr_lr = apply_axial_rope(kr_l, cos, sin)
    q = split_heads(q_l, h)
    qn, qr = q[..., :MLA_NOPE], apply_axial_rope(q[..., MLA_NOPE:], cos, sin)
    kn = jnp.concatenate([kn_c, kn_l], axis=2)
    kr = jnp.concatenate([kr_c, kr_lr], axis=1)
    v = jnp.concatenate([v_c, v_l], axis=2)
    b, _, n, _ = qn.shape
    nb = n // Q_BLOCK

    def block(qs):
        qn_b, qr_b = qs
        s = (jnp.einsum("bhqd,bhkd->bhqk", qn_b, kn)
             + jnp.einsum("bhqd,bkd->bhqk", qr_b, kr)).astype(jnp.float32) * scale
        p = softmax_f32(s)
        return jnp.einsum("bhqk,bhkd->bhqd", p.astype(v.dtype), v)

    to_blocks = lambda t: t.reshape(b, h, nb, Q_BLOCK, t.shape[-1]).transpose(2, 0, 1, 3, 4)
    o = lax.map(block, (to_blocks(qn), to_blocks(qr)))
    y_l = merge_heads(o.transpose(1, 2, 0, 3, 4).reshape(b, h, n, MLA_V))
    y_c = None
    if with_ctx:
        qc = split_heads(q_c, h)
        kc = jnp.concatenate([kn_c, jnp.broadcast_to(kr_c[:, None], kn_c.shape[:3] + (MLA_ROPE,))], axis=-1)
        y_c = merge_heads(dense_ctx_attention(qc, kc, v_c, scale))
    return y_l, y_c

def swa_mixer(q_l, k_l, v_l, q_c, k_c, v_c, sink, cos, sin, with_ctx):
    h, g = GROUP_HEADS, SWA_KV_HEADS
    r = h // g
    d = HEAD_DIM
    scale = d ** -0.5
    q = apply_axial_rope(split_heads(q_l, h), cos, sin)
    k = apply_axial_rope(split_heads(k_l, g), cos, sin)
    v = split_heads(v_l, g)
    kc, vc = split_heads(k_c, g), split_heads(v_c, g)
    b, _, n, _ = q.shape
    nb = n // SWA_BLOCK
    qb = q.reshape(b, g, r, nb, SWA_BLOCK, d)

    def band(t):
        tb = t.reshape(b, g, nb, SWA_BLOCK, d)
        tp = jnp.pad(tb, ((0, 0), (0, 0), (1, 1), (0, 0), (0, 0)))
        return jnp.concatenate([tp[:, :, :-2], tp[:, :, 1:-1], tp[:, :, 2:]], axis=3)

    kband, vband = band(k), band(v)
    nk = 3 * SWA_BLOCK
    rel = np.arange(nk)[None, :] - SWA_BLOCK - np.arange(SWA_BLOCK)[:, None]
    kpos = (np.arange(nb)[:, None] - 1) * SWA_BLOCK + np.arange(nk)[None, :]
    mask = (np.abs(rel) <= SWA_WINDOW)[None] & ((kpos >= 0) & (kpos < n))[:, None, :]
    s_band = jnp.einsum("bgrnqd,bgnkd->bgrnqk", qb, kband).astype(jnp.float32) * scale
    s_band = jnp.where(mask, s_band, NEG_INF)
    s_ctx = jnp.einsum("bgrnqd,bgkd->bgrnqk", qb, kc).astype(jnp.float32) * scale
    sink_col = jnp.broadcast_to(sink.astype(jnp.float32).reshape(1, g, r, 1, 1, 1), s_ctx.shape[:-1] + (1,))
    p = softmax_f32(jnp.concatenate([s_band, s_ctx, sink_col], axis=-1))
    n_ctx = kc.shape[2]
    o = (jnp.einsum("bgrnqk,bgnkd->bgrnqd", p[..., :nk].astype(v.dtype), vband)
         + jnp.einsum("bgrnqk,bgkd->bgrnqd", p[..., nk:nk + n_ctx].astype(v.dtype), vc))
    y_l = merge_heads(o.reshape(b, h, n, d))
    y_c = None
    if with_ctx:
        y_c = merge_heads(dense_ctx_attention(split_heads(q_c, h), jnp.repeat(kc, r, axis=1),
                                              jnp.repeat(vc, r, axis=1), scale, sink))
    return y_l, y_c

def na_mixer(q_l, k_l, v_l, q_c, k_c, v_c, rpb, with_ctx):
    h, d = GROUP_HEADS, HEAD_DIM
    scale = d ** -0.5
    q, k, v = split_heads(q_l, h), split_heads(k_l, h), split_heads(v_l, h)
    kc, vc = split_heads(k_c, h), split_heads(v_c, h)
    b, _, n, _ = q.shape
    rows = n // GRID_W
    kh = min(NA_KH, rows)
    nj = GRID_W // NA_QB_W
    qcol = np.arange(GRID_W).reshape(nj, NA_QB_W)
    cs = np.clip(qcol - NA_KW // 2, 0, GRID_W - NA_KW)
    cb = np.minimum(cs[:, 0], GRID_W - NA_KB_W)
    kcol = cb[:, None] + np.arange(NA_KB_W)[None, :]
    col_mask = (kcol[:, None, :] >= cs[:, :, None]) & (kcol[:, None, :] < cs[:, :, None] + NA_KW)
    dc_idx = np.clip(kcol[:, None, :] - qcol[:, :, None] + NA_KW - 1, 0, 2 * NA_KW - 2).astype(np.int32)
    r_idx = np.arange(rows)
    rs = np.clip(r_idx - kh // 2, 0, rows - kh)
    dr_idx = (rs[:, None] + np.arange(kh)[None, :] - r_idx[:, None] + NA_KH - 1).astype(np.int32)
    kg = k.reshape(b, h, rows, GRID_W, d)
    vg = v.reshape(b, h, rows, GRID_W, d)
    qg = q.reshape(b, h, rows, GRID_W, d).transpose(2, 0, 1, 3, 4)
    rpb_f = rpb.astype(jnp.float32)
    nk = kh * NA_KB_W

    def row_block(inp):
        q_row, r0, dri = inp
        k_win = lax.dynamic_slice_in_dim(kg, r0, kh, axis=2)[:, :, :, kcol]
        v_win = lax.dynamic_slice_in_dim(vg, r0, kh, axis=2)[:, :, :, kcol]
        qb = q_row.reshape(b, h, nj, NA_QB_W, d)
        s = jnp.einsum("bhjqd,bhajkd->bhjqak", qb, k_win).astype(jnp.float32) * scale
        bias = rpb_f[:, dri][:, :, dc_idx].transpose(0, 2, 3, 1, 4)
        s = jnp.where(col_mask[:, :, None, :], s + bias, NEG_INF).reshape(b, h, nj, NA_QB_W, nk)
        s_ctx = jnp.einsum("bhjqd,bhkd->bhjqk", qb, kc).astype(jnp.float32) * scale
        p = softmax_f32(jnp.concatenate([s, s_ctx], axis=-1))
        p_win = p[..., :nk].reshape(b, h, nj, NA_QB_W, kh, NA_KB_W).astype(v.dtype)
        o = (jnp.einsum("bhjqak,bhajkd->bhjqd", p_win, v_win)
             + jnp.einsum("bhjqk,bhkd->bhjqd", p[..., nk:].astype(v.dtype), vc))
        return o.reshape(b, h, GRID_W, d)

    o = lax.map(row_block, (qg, jnp.asarray(rs, jnp.int32), jnp.asarray(dr_idx)))
    y_l = merge_heads(o.transpose(1, 2, 0, 3, 4).reshape(b, h, n, d))
    y_c = None
    if with_ctx:
        y_c = merge_heads(dense_ctx_attention(split_heads(q_c, h), kc, vc, scale))
    return y_l, y_c

def retention_scan(q, k, v, log_gamma, state0, emit):
    b, h, t, _ = q.shape
    c = RET_CHUNK
    nc = t // c
    idx = jnp.arange(c, dtype=jnp.float32)
    diff = idx[:, None] - idx[None, :]
    lg = log_gamma[:, None, None]
    decay_in = jnp.where(diff >= 0, jnp.exp(lg * jnp.maximum(diff, 0.0)), 0.0)
    q_dec = jnp.exp(log_gamma[:, None] * (idx + 1.0))[..., None]
    k_dec = jnp.exp(log_gamma[:, None] * (c - 1.0 - idx))[..., None]
    c_dec = jnp.exp(log_gamma * c)[:, None, None]
    chunks = lambda a: a.reshape(b, h, nc, c, a.shape[-1]).transpose(2, 0, 1, 3, 4)

    def step(s, inp):
        qb, kb, vb = inp
        s_new = s * c_dec + jnp.einsum("bhjd,bhje->bhde", kb * k_dec, vb)
        if emit:
            inner = jnp.einsum("bhid,bhjd->bhij", qb, kb) * decay_in
            o = jnp.einsum("bhij,bhjd->bhid", inner, vb) + jnp.einsum("bhid,bhde->bhie", qb * q_dec, s)
            return s_new, o
        return s_new, None

    s_fin, o = lax.scan(step, state0, (chunks(q), chunks(k), chunks(v)))
    if emit:
        o = o.transpose(1, 2, 0, 3, 4).reshape(b, h, t, -1)
    return o, s_fin

def head_groupnorm(o, g):
    mu = jnp.mean(o, axis=-1, keepdims=True)
    var = jnp.mean(jnp.square(o - mu), axis=-1, keepdims=True)
    return merge_heads((o - mu) * lax.rsqrt(var + EPS)) * g.astype(jnp.float32)

def retention_gate(o_f, o_b, g_f, g_b, gn_f, gn_b):
    y = (jax.nn.silu(g_f.astype(jnp.float32)) * head_groupnorm(o_f, gn_f)
         + jax.nn.silu(g_b.astype(jnp.float32)) * head_groupnorm(o_b, gn_b))
    return y.astype(g_f.dtype)

def retention_mixer(q_l, k_l, v_l, gf_l, gb_l, q_c, k_c, v_c, gf_c, gb_c,
                    decay_f, decay_b, gn_f, gn_b, with_ctx):
    prep = lambda t: split_heads(t, GROUP_HEADS).astype(jnp.float32)
    kscale = HEAD_DIM ** -0.5
    ql, kl, vl = prep(q_l), prep(k_l) * kscale, prep(v_l)
    qc, kc, vc = prep(q_c), prep(k_c) * kscale, prep(v_c)
    lg_f = jax.nn.log_sigmoid(decay_f.astype(jnp.float32))
    lg_b = jax.nn.log_sigmoid(decay_b.astype(jnp.float32))
    zero = jnp.zeros(kl.shape[:2] + (HEAD_DIM, HEAD_DIM), jnp.float32)
    flip = lambda t: t[:, :, ::-1]
    oc_f, s_f = retention_scan(qc, kc, vc, lg_f, zero, with_ctx)
    oc_b, s_b = retention_scan(flip(qc), flip(kc), flip(vc), lg_b, zero, with_ctx)
    ol_f, _ = retention_scan(ql, kl, vl, lg_f, s_f, True)
    ol_b, _ = retention_scan(flip(ql), flip(kl), flip(vl), lg_b, s_b, True)
    y_l = retention_gate(ol_f, flip(ol_b), gf_l, gb_l, gn_f, gn_b)
    y_c = None
    if with_ctx:
        y_c = retention_gate(oc_f, flip(oc_b), gf_c, gb_c, gn_f, gn_b)
    return y_l, y_c

def peer_ffn(hid, wq, sub_k1, sub_k2, expert_u, expert_v):
    b, t, d = hid.shape
    flat = hid.reshape(b * t, d)
    blk = math.gcd(b * t, PEER_TOKEN_BLOCK)
    half = PEER_DKEY // 2

    def block(xb):
        tb = xb.shape[0]
        q = (xb @ wq).reshape(tb, PEER_HEADS, 2, half).astype(jnp.float32)
        s1 = jnp.einsum("thd,nd->thn", q[:, :, 0], sub_k1.astype(jnp.float32))
        s2 = jnp.einsum("thd,nd->thn", q[:, :, 1], sub_k2.astype(jnp.float32))
        v1, i1 = lax.top_k(s1, PEER_TOPK)
        v2, i2 = lax.top_k(s2, PEER_TOPK)
        cand_s = (v1[..., :, None] + v2[..., None, :]).reshape(tb, PEER_HEADS, PEER_TOPK * PEER_TOPK)
        cand_i = (i1[..., :, None] * PEER_NKEYS + i2[..., None, :]).reshape(tb, PEER_HEADS, PEER_TOPK * PEER_TOPK)
        top_s, pos = lax.top_k(cand_s, PEER_TOPK)
        eid = jnp.take_along_axis(cand_i, pos, axis=-1).reshape(tb, PEER_HEADS * PEER_TOPK)
        gate = jax.nn.softmax(top_s, axis=-1).reshape(tb, PEER_HEADS * PEER_TOPK)
        a = jnp.einsum("td,tkd->tk", xb, expert_u[eid]).astype(jnp.float32)
        w = (jax.nn.gelu(a, approximate=False) * gate).astype(xb.dtype)
        return jnp.einsum("tk,tkd->td", w, expert_v[eid])

    out = lax.map(block, flat.reshape(-1, blk, d))
    return out.reshape(b, t, d)

def setup_inputs(seed: int = 0) -> dict:
    key = jax.random.key(seed)
    ks = jax.random.split(key, 26)
    f32 = jnp.float32
    L, D, H = DEPTH, D_MODEL, GROUP_HEADS
    nrm = lambda k, shape, s: jax.random.normal(k, shape, f32) * s
    gain = lambda k, shape: 1.0 + 0.02 * jax.random.normal(k, shape, f32)
    decay0 = jnp.asarray(np.log(2.0 ** (5 + np.arange(H)) - 1.0), f32)
    return {
        "x": nrm(ks[0], (BATCH, SEQ, D), 1.0),
        "c": nrm(ks[1], (BATCH, D), 1.0),
        "ctx": nrm(ks[2], (BATCH, CTX_LEN, D), 1.0),
        "c_ctx": nrm(ks[3], (D,), 1.0),
        "ada_w": nrm(ks[4], (L, D, ADA_CHUNKS * D), 0.5 * D ** -0.5),
        "ada_b": nrm(ks[5], (L, ADA_CHUNKS * D), 0.01),
        "norm_mix_g": gain(ks[6], (L, D)),
        "w_in": nrm(ks[7], (L, D, IN_WIDTH), D ** -0.5),
        "mla_kv_norm_g": gain(ks[8], (L, MLA_KV_RANK)),
        "mla_w_ukv": nrm(ks[9], (L, MLA_KV_RANK, H * (MLA_NOPE + MLA_V)), MLA_KV_RANK ** -0.5),
        "swa_sink": nrm(ks[10], (L, H), 0.5),
        "na_rpb": nrm(ks[11], (L, H, 2 * NA_KH - 1, 2 * NA_KW - 1), 0.1),
        "ret_decay_f": decay0 + nrm(ks[12], (L, H), 0.1),
        "ret_decay_b": decay0 + nrm(ks[13], (L, H), 0.1),
        "ret_gn_f": gain(ks[14], (L, GROUP_WIDTH)),
        "ret_gn_b": gain(ks[15], (L, GROUP_WIDTH)),
        "mix_beta": gain(ks[16], (L, D)),
        "w_out": nrm(ks[17], (L, D, D), D ** -0.5),
        "norm_ffn_g": gain(ks[18], (L, D)),
        "peer_wq": nrm(ks[19], (L, D, PEER_HEADS * PEER_DKEY), D ** -0.5),
        "peer_k1": nrm(ks[20], (L, PEER_NKEYS, PEER_DKEY // 2), (PEER_DKEY // 2) ** -0.5),
        "peer_k2": nrm(ks[21], (L, PEER_NKEYS, PEER_DKEY // 2), (PEER_DKEY // 2) ** -0.5),
        "peer_u": nrm(ks[22], (L, PEER_EXPERTS, D), D ** -0.5),
        "peer_v": nrm(ks[23], (L, PEER_EXPERTS, D), 0.5),
        "final_norm_g": gain(ks[24], (D,)),
    }

def reference(x, c, ctx, c_ctx, ada_w, ada_b, norm_mix_g, w_in, mla_kv_norm_g, mla_w_ukv, swa_sink, na_rpb,
              ret_decay_f, ret_decay_b, ret_gn_f, ret_gn_b, mix_beta, w_out, norm_ffn_g, peer_wq, peer_k1,
              peer_k2, peer_u, peer_v, final_norm_g):
    n = x.shape[1]
    cos_r, sin_r = axial_rope_tables(n, MLA_ROPE)
    cos_h, sin_h = axial_rope_tables(n, HEAD_DIM)
    cuts = np.cumsum(IN_SPLITS)[:-1].tolist()
    xc = ctx
    for layer in range(DEPTH):
        with_ctx = layer < DEPTH - 1
        mod_l = jnp.split(jax.nn.silu(c) @ ada_w[layer] + ada_b[layer], ADA_CHUNKS, axis=-1)
        mod_c = jnp.split(jax.nn.silu(c_ctx)[None, :] @ ada_w[layer] + ada_b[layer], ADA_CHUNKS, axis=-1)
        p_l = jnp.split(modulate(rmsnorm(x, norm_mix_g[layer]), mod_l[0], mod_l[1]) @ w_in[layer], cuts, axis=-1)
        p_c = jnp.split(modulate(rmsnorm(xc, norm_mix_g[layer]), mod_c[0], mod_c[1]) @ w_in[layer], cuts, axis=-1)
        ya_l, ya_c = mla_mixer(*p_l[0:3], *p_c[0:3], mla_kv_norm_g[layer], mla_w_ukv[layer], cos_r, sin_r, with_ctx)
        yb_l, yb_c = swa_mixer(*p_l[3:6], *p_c[3:6], swa_sink[layer], cos_h, sin_h, with_ctx)
        yc_l, yc_c = na_mixer(*p_l[6:9], *p_c[6:9], na_rpb[layer], with_ctx)
        yd_l, yd_c = retention_mixer(*p_l[9:14], *p_c[9:14], ret_decay_f[layer], ret_decay_b[layer],
                                     ret_gn_f[layer], ret_gn_b[layer], with_ctx)
        y_l = jnp.concatenate([ya_l, yb_l, yc_l, yd_l], axis=-1) * mix_beta[layer]
        x = x + mod_l[2][:, None, :] * (y_l @ w_out[layer])
        h2 = modulate(rmsnorm(x, norm_ffn_g[layer]), mod_l[3], mod_l[4])
        x = x + mod_l[5][:, None, :] * peer_ffn(h2, peer_wq[layer], peer_k1[layer], peer_k2[layer],
                                                 peer_u[layer], peer_v[layer])
        if with_ctx:
            y_c = jnp.concatenate([ya_c, yb_c, yc_c, yd_c], axis=-1) * mix_beta[layer]
            xc = xc + mod_c[2][:, None, :] * (y_c @ w_out[layer])
            h2c = modulate(rmsnorm(xc, norm_ffn_g[layer]), mod_c[3], mod_c[4])
            xc = xc + mod_c[5][:, None, :] * peer_ffn(h2c, peer_wq[layer], peer_k1[layer], peer_k2[layer],
                                                       peer_u[layer], peer_v[layer])
    return rmsnorm(x, final_norm_g)


_drawn_inputs = setup_inputs


def setup_inputs(seed=0):
    import zlib

    import numpy as np

    out = dict(_drawn_inputs(seed))
    spreads = {}
    factors = {'ada_b': 2.798,
     'norm_mix_g': 4.054,
     'mla_kv_norm_g': 8.0,
     'swa_sink': 8.0,
     'na_rpb': 8.0,
     'ret_gn_f': 7.492,
     'ret_gn_b': 7.307,
     'mix_beta': 5.813,
     'norm_ffn_g': 24.704,
     'final_norm_g': 8.216}
    for name, (base, spread) in spreads.items():
        noise = np.random.default_rng([zlib.crc32(name.encode()), seed]).standard_normal(out[name].shape)
        drawn = base * np.exp(spread * noise) if base else spread * noise
        out[name] = jnp.asarray(drawn.astype(out[name].dtype))
    for name, factor in factors.items():
        out[name] = (out[name] * factor).astype(out[name].dtype)
    return out
```

```python
from contextlib import ExitStack

import numpy as np

import concourse.bass as bass
from concourse import mybir

F32 = mybir.dt.float32
U32 = mybir.dt.uint32
ALU = mybir.AluOpType
ACT = mybir.ActivationFunctionType
AX = mybir.AxisListType.X

P = 128
D = 1024
KD = D // P
LAYERS = 2
NCTX, NLAT = 256, 512
TILES = (NCTX + NLAT) // P
CT = NCTX // P
TOK = NCTX + NLAT
HEADS, HD = 4, 64
GW = HEADS * HD
MLA_QK = 96
GRID = 64
ROWS = NLAT // GRID
NA_PITCH = 48
IN_WIDTH = 3104
C_QCKV, C_KR, C_SWA, C_NAQK, C_NAV_RQ, C_RKV, C_GATE = 0, 512, 544, 1056, 1568, 2080, 2592
IN_CHUNKS = (C_QCKV, C_SWA, C_NAQK, C_NAV_RQ, C_RKV, C_GATE)
CH = 512
GROUP_K = 4
WRING = 3
ADA_CHUNKS = 6 * D // CH
PH, NKEYS, TOPK = 8, 128, 16
SLOTS = PH * TOPK
EXPERTS = NKEYS * NKEYS
EPS = 1e-6
NEG = -1e30
MLA_SCALE = float(MLA_QK) ** -0.5
CHOOSE_EVERY = 2
CHOOSE_STEPS = 23
GATES_AT = 54
UVRING = 11
BATCH = 2


def col_starts():
    first = np.clip(np.arange(4) * 16 - 8, 0, GRID - 16)
    return [int(v) for v in np.minimum(first, GRID - 32)]


def na_mask():
    out = np.zeros((4, P, ROWS, 32), np.float32)
    p = np.arange(P)
    for j, cb in enumerate(col_starts()):
        q = 16 * j + 8 * (p // HD) + p % 8
        cs = np.clip(q - 8, 0, GRID - 16)[:, None]
        k = cb + np.arange(32)[None, :]
        ok = (k >= cs) & (k < cs + 16)
        out[j] = np.where(ok, 0.0, NEG)[:, None, :]
    return out.reshape(4, P, ROWS, 4, 8).transpose(0, 1, 3, 2, 4).reshape(4, P, 256)


def constants():
    i = np.arange(P)
    diff = (i[None, :] - i[:, None]).astype(np.float32)
    ret = np.stack([np.maximum(diff, 0), np.maximum(-diff, 0), (diff >= 0), (diff <= 0)], 1).astype(np.float32)
    pos = np.zeros((P, 2, P), np.float32)
    pos[:, 0], pos[:, 1] = i + 1, P - i
    kpos = np.zeros((P, 8), np.float32)
    kpos[:, :4], kpos[:, 4:] = (P - 1 - i)[:, None], i[:, None]
    blk = (i[:, None] // HD == i[None, :] // HD).astype(np.float32)
    swa = np.stack([np.where(diff >= 0, 0, NEG)[:, :], np.where(diff <= 0, 0, NEG)], 1).astype(np.float32)
    tok = np.arange(NLAT)
    grid = np.stack([tok // GRID, tok % GRID], -1).astype(np.float32)

    def rope(dim):
        quarter = dim // 4
        inv = np.float32(10000.0) ** (-np.arange(quarter, dtype=np.float32) / np.float32(quarter))
        ang = (grid[:, :, None] * inv.astype(np.float32)).astype(np.float32)
        both = np.stack([np.cos(ang), np.sin(ang)], 1).astype(np.float32)
        return both.reshape(NLAT // P, P, 4 * quarter).transpose(1, 0, 2)

    return {
        "c_ident": np.eye(P, dtype=np.float32),
        "c_ret": ret.reshape(P, 4 * P),
        "c_pos": np.concatenate([pos.reshape(P, 2 * P), kpos, blk], 1),
        "c_swa": swa.reshape(P, 2 * P),
        "c_na": na_mask().transpose(1, 0, 2).reshape(P, 4 * 256).copy(),
        "c_rope16": np.ascontiguousarray(rope(32).reshape(P, -1)),
        "c_rope32": np.ascontiguousarray(rope(64).reshape(P, -1)),
        "c_iota": np.tile(np.arange(TOPK, dtype=np.float32), (P, 1)),
    }


class Chain:

    def __init__(self, eng, sem):
        self.eng, self.sem, self.n, self.turns = eng, sem, 0, 0

    def __call__(self, ins):
        self.n += 1
        ins.then_inc(self.sem, 1)
        self.eng.wait_ge(self.sem, self.turns + self.n)

    def then_max(self, ins):
        self(ins)
        self.eng.sem_inc(self.own, 1)

    def loop(self, first, end, per):
        before = self.n
        with self.eng.Fori(first, end) as i:
            self.turns = (i - first) * per
            yield i
        assert self.n == before + per, self.n - before
        self.turns, self.n = 0, before + per * (end - first)


def attention_items(kind, layer):
    items = []
    for t in range(CT if layer == LAYERS - 1 else 0, TILES):
        for h in range(HEADS):
            if t < CT:
                spans = [(0, NCTX)]
            elif kind == "mla":
                spans = [(0, TOK)]
            elif kind == "swa":
                lo, hi = max(t - 1, CT), min(t + 2, TILES)
                spans = [(0, NCTX), (lo * P, (hi - lo) * P)]
            else:
                spans = [(0, NCTX), (NCTX + ROWS * col_starts()[t - CT], 256)]
            items.append((t, h, spans))
    return items


def first_layer_counts():
    c = {}
    for value, names in (
        (TILES, "c0 c0r c1 c1r c4 c4e c5 c5d c5e ckn ckr cks kd qe qt rke rkt sqe sqt u vme vmm "
                "ge gx gr gv oc inner pfb ro ry rye ryt topk istg stg xa xf"),
        (2 * TILES, "op og xo"),
        (4, "c2 c2e c3 c3e"),
        (HEADS, "kn kne qd qdt"),
        (1, "cd cke ckq ckt dabs dex dln kr krc kre krr krt krz kte lg kd8 st"),
        (2 * HEADS, "dt dtm"),
        (2 * PH, "fq fqe fs fse"),
        (ADA_CHUNKS, "mps mrow"),
        (4 * HEADS, "nb"),
        (16 * 2, "nt rtab gt gt2"),
        (16 * 8, "small"),
        (TILES - CT, "rope rop2"),
        (CT + 7, "vne vnt"),
        (16 * ADA_CHUNKS // 2, "ms0 ms1 ab0 ab1"),
        (16 * PH, "sd0 sd1"),
        (16 * TILES, "sl"),
        (TILES * SLOTS, "dg em"),
        (TILES * SLOTS // BATCH, "dot gel"),
    ):
        for name in names.split():
            c[name] = value
    for r in range(UVRING):
        c[f"uv{r}"] = 16 * TILES * slot_uses(r)
    return c


def slot_uses(r):
    return (SLOTS - 1 - r) // UVRING + 1


def att_base(kind, layer):
    per = [HEADS * TILES, HEADS * (TILES - CT)]
    return 3 * per[0] * layer + ("mla", "swa", "na").index(kind) * per[layer]


def nb_(which, layer):
    return 2 * TILES * layer + TILES * which


def width(spans):
    return sum(w for _, w in spans)


def build(nc, a, out):
    ctx = ExitStack()
    with ctx:
        def sb(name, shape, dt=F32):
            return ctx.enter_context(nc.sbuf_tensor(name, shape, dt))

        sems = {}

        def S(name):
            if name not in sems:
                sems[name] = ctx.enter_context(nc.semaphore(name))
            return sems[name]

        xs = sb("xs", [P, TILES, D])
        hT = sb("hT", [P, KD, TOK])
        yT = sb("yT", [P, KD, TOK])
        wring = sb("wring", [P, WRING, GROUP_K, CH])
        ident = sb("ident", [P, P])
        wkr = sb("wkr", [P, KD, 32])
        wukv = sb("wukv", [P, 512])
        keysT = sb("keysT", [P, 2, NKEYS])
        gkv = sb("gkv", [P, P])
        beta = sb("beta", [P, KD])
        smallw = sb("smallw", [P, 16])
        rope16 = sb("rope16", [P, 4, 2, 2, 8])
        rope32 = sb("rope32", [P, 4, 2, 2, 16])
        swam = sb("swam", [P, 2, P])
        iota = sb("iota", [P, TOPK])
        cT = sb("cT", [P, KD, 2])
        cE = sb("cE", [P, KD, 2])
        eps = sb("eps", [P, 1])
        stat = sb("stat", [P, 4, 8])
        att = sb("att", [P, 6, 32])
        X_WORDS = 101 * 256
        X = sb("X", [P, X_WORDS])
        ps = ctx.enter_context(nc.psum_tensor("ps", [P, 8, 512], F32))

        def view(at, shape, dt=None):
            n = int(np.prod(shape))
            assert at + n <= X_WORDS, (at, shape)
            v = X[:, at:at + n]
            if dt is not None:
                v = v.bitcast(dt)
            if len(shape) == 2:
                v = v.rearrange("p (a b) -> p a b", b=shape[1])
            elif len(shape) == 3:
                v = v.rearrange("p (a b c) -> p a b c", b=shape[1], c=shape[2])
            elif len(shape) == 4:
                v = v.rearrange("p (a b c d) -> p a b c d", b=shape[1], c=shape[2], d=shape[3])
            return v

        K = 256
        qm = view(0, [HEADS, TOK]); km = view(12 * K, [HEADS, TOK]); vm = view(24 * K, [TILES, GW])
        sq = view(30 * K, [2, TOK]); sk = view(36 * K, [1, TOK]); vs = view(39 * K, [TILES, P])
        nq = view(42 * K, [2, TOK]); nk = view(48 * K, [2, TOK]); vn = view(54 * K, [9, GW])
        nbias = view(63 * K, [2, 256]); rpbt = view(65 * K, [HEADS, ROWS, NA_PITCH]); nmask = view(71 * K, [4, 256])
        pr = view(75 * K, [2, TOK]); pT = view(81 * K, [2, TOK])
        prow = view(87 * K, [3, CH]); yr = view(93 * K, [2, GW])
        ckvT = view(63 * K, [TOK]); ckv = view(66 * K, [TILES, P])
        rq = view(0, [2, TOK]); rk = view(6 * K, [2, TOK]); rkr = view(12 * K, [TILES, GW])
        rv = view(18 * K, [TILES, GW]); gate = view(24 * K, [TILES, 2 * GW])
        qd = view(42 * K, [2, 2, TOK]); dt_ = view(54 * K, [2, HEADS, P]); rtab = view(58 * K, [4, P])
        st = view(60 * K, [TILES, 4, P]); qdt = view(72 * K, [2, 2, P])
        pfb = view(75 * K, [2, 2, HEADS * P]); kd = view(83 * K, [2, 2, GW])
        on = view(87 * K, [2, 2 * GW]); osq = view(91 * K, [2 * GW]); gn = view(93 * K, [2 * GW])
        tabs = view(42 * K, [4, D]); gbc = view(58 * K, [D]); hrow = view(62 * K, [2, D]); junk = view(70 * K, [D])
        mrow = view(87 * K, [2, CH]); adab = view(91 * K, [2, CH])
        ptab = sb("ptab", [P, 2 * P + 8 + P])
        krrow = view(69 * K, [TILES, MLA_QK])
        rsm = sb("rsm", [P, 64])
        qTb = view(48 * K, [2, TOK]); stage = view(54 * K, [2, TOK])
        uvr = view(0, [UVRING, 2 * D])
        scn = view(88 * K, [2 * PH, NKEYS])
        tk = view(96 * K, [2, NKEYS]); cand = view(97 * K, [TOPK, TOPK]); cand2 = view(98 * K, [TOPK * TOPK])
        oh = view(99 * K, [TOPK, TOPK]); v12 = view(100 * K, [2, TOPK]); i12 = view(100 * K + 32, [2, TOPK], U32)
        i12f = view(100 * K + 64, [2, TOPK]); pos = view(100 * K + 96, [TOPK], U32); pab = view(100 * K + 112, [2, TOPK], U32)
        pabf = view(100 * K + 144, [2, TOPK]); sel = view(100 * K + 176, [2, TOPK]); gs = view(100 * K + 208, [2, PH])
        hflat = hT[:, :, :].rearrange("p a b -> p (a b)")
        h2 = yT[:, :, :].rearrange("p a b -> p (a b)").rearrange("p (t d) -> p t d", d=D)
        xt = hflat[:, 0:D]; gjunk = hflat[:, D:2 * D]; gtab = hflat[:, 2 * D:4 * D].rearrange("p (a b) -> p a b", b=D)
        dg = hflat[:, 4 * D:5 * D].rearrange("p (a b) -> p a b", b=P)
        small = hflat[:, 5 * D:6 * D]
        adot = small[:, 0:SLOTS]; agel = small[:, SLOTS:2 * SLOTS]
        gstage = small[:, 2 * SLOTS:3 * SLOTS]; istage = small[:, 3 * SLOTS:4 * SLOTS].bitcast(U32)
        top = small[:, 4 * SLOTS:5 * SLOTS].rearrange("p (h k) -> p h k", k=TOPK)
        gx = small[:, 5 * SLOTS:7 * SLOTS].rearrange("p (a b) -> p a b", b=SLOTS)
        idxn = small[:, 7 * SLOTS:8 * SLOTS].rearrange("p (h k) -> p h k", k=TOPK)

        counts = first_layer_counts()

        def B(name, layer):
            return counts[name] if layer else 0

        scores_d = nc.dram_tensor("scores", (TILES, P, 2 * PH, NKEYS), F32, kind="Internal").ap()
        mods = nc.dram_tensor("mods", (LAYERS, 2, 6 * D), F32, kind="Internal").ap()

        block = ctx.enter_context(nc.Block())
        LAST = LAYERS - 1
        first_out = [0, CT]

        @block.sync
        def _(sp):
            sp.dma_start(cT[:, :, :], a["c"]).then_inc(S("in"), 16)
            sp.dma_start(ident[:, :], a["c_ident"]).then_inc(S("in"), 16)
            sp.dma_start(xs[:, 0:CT, :], a["ctx"].rearrange("(t p) d -> p t d", p=P)).then_inc(S("in"), 16)
            sp.dma_start(xs[:, CT:TILES, :], a["x"].rearrange("(t p) d -> p t d", p=P)).then_inc(S("in"), 16)
            sp.dma_start(swam[:, :, :], a["c_swa"].rearrange("p (a b) -> p a b", b=P)).then_inc(S("in"), 16)
            sp.dma_start(ptab[:, :], a["c_pos"]).then_inc(S("in"), 16)
            sp.dma_start(rope16[:, :, :, :, :].rearrange("p a b c d -> p (a b c d)"), a["c_rope16"]).then_inc(S("in"), 16)
            sp.dma_start(rope32[:, :, :, :, :].rearrange("p a b c d -> p (a b c d)"), a["c_rope32"]).then_inc(S("in"), 16)
            sp.dma_start(iota[:, :], a["c_iota"]).then_inc(S("in"), 16)

            done, halves = [], 0
            for L in range(LAYERS):
                made = TILES - first_out[L]
                stream = [(a["ada_w"][L], D6, "mps", c + 1, True) for c, D6 in enumerate(range(0, 6 * D, CH))]
                stream += [(a["w_in"][L], col, name, count, split) for col, name, count, split in (
                    (C_QCKV, "c0", TILES, True), (C_SWA, "c1", TILES, True), (C_NAQK, "c2", 4, False),
                    (C_NAV_RQ, "c3", 4, False), (C_RKV, "c4", TILES, True), (C_GATE, "c5", TILES, True))]
                stream += [(a["w_out"][L], c * CH, "op", (c + 1) * made, True) for c in range(2)]
                stream += [(a["peer_wq"][L], c * CH, "fq", 4 * (c + 1), False) for c in range(4)]
                for w, col, name, count, split in stream:
                    for half in range(2):
                        g = len(done)
                        if g >= WRING:
                            sp.wait_ge(S(done[g - WRING][0]), done[g - WRING][1])
                        k0 = half * GROUP_K
                        src = w.rearrange("(k p) n -> p k n", p=P)[:, k0:k0 + GROUP_K, col:col + CH]
                        sp.dma_start(wring[:, g % WRING, :, :], src).then_inc(S(f"w{g % WRING}"), 16)
                        if split and half == 0:
                            halves += 1
                            done.append(("w_half", halves))
                        else:
                            done.append((name, B(name, L) + count))
                lo = first_out[L]
                for q in range(2):
                    sp.wait_ge(S(f"sd{q}"), B(f"sd{q}", L) + 16 * PH)
                sp.dma_start(scn, scores_d[lo]).then_inc(S("sl"), 16)
                with sp.Fori(0, TILES - lo - 1) as i:
                    sp.wait_ge(S("topk"), B("topk", L) + i + 1)
                    sp.dma_start(scn, scores_d[bass.ds(i + lo + 1, 1)].rearrange("t p j n -> p (t j) n")).then_inc(S("sl"), 16)
            for t in range(TILES - CT):
                sp.wait_ge(S("fin"), t + 1)
                sp.dma_start(out[t * P:(t + 1) * P, :], xs[:, CT + t, :]).then_inc(S("out"), 16)
            sp.wait_ge(S("out"), 16 * (TILES - CT))

        @block.tensor
        def _(pe):
            pe.wait_ge(S("in"), 16 * 9)
            wg = [0]

            def take(n=2):
                g = wg[0]
                for i in range(n):
                    pe.wait_ge(S(f"w{(g + i) % WRING}"), 16 * ((g + i) // WRING + 1))
                wg[0] += n
                return g

            def wsl(g, k, c0, c1):
                return wring[:, (g + k // GROUP_K) % WRING, k % GROUP_K, c0:c1]

            def rows_chunk(L, tiles, ready):
                for half in range(2):
                    g = take(1)
                    for kk in range(GROUP_K):
                        k = half * GROUP_K + kk
                        for t in tiles:
                            m = pe.matmul(ps[:, t, :], hT_or_y[0][:, k, t * P:(t + 1) * P],
                                          wring[:, g % WRING, kk, :], start=(k == 0), stop=(k == KD - 1))
                            if k == KD - 1 and t != tiles[-1]:
                                m.then_inc(ready, 1)
                    if half == 0:
                        m.then_inc(S("w_half"), 1)
                m.then_inc(ready, 1)

            hT_or_y = [hT]
            for L in range(LAYERS):
                n = f"_{L}"
                lo = first_out[L]
                if L:
                    pe.wait_ge(S("layer"), L)
                pe.wait_ge(S("silu"), 1)
                for c in range(ADA_CHUNKS):
                    g = take(2)
                    if c >= 2:
                        pe.wait_ge(S("mrow"), B("mrow", L) + c - 1)
                    for k in range(KD):
                        m = pe.matmul(ps[0:2, c % 2, :], cT[:, k, :], wsl(g, k, 0, CH), start=(k == 0), stop=(k == KD - 1))
                        if k == GROUP_K - 1:
                            m.then_inc(S("w_half"), 1)
                    m.then_inc(S("mps"), 1)

                def norm_transposes(tag, tiles, rows):
                    for i, t in enumerate(tiles):
                        pe.wait_ge(S("n_h"), nb_(tag, L) + i + 1)
                        if i >= 2:
                            pe.wait_ge(S("n_hT"), nb_(tag, L) + i - 1)
                        else:
                            pe.wait_ge(S("mrow"), B("mrow", L) + ADA_CHUNKS)
                        for k in range(KD):
                            m = pe.transpose(ps[:, 2 * (i % 2) + k // 4, (k % 4) * P:(k % 4 + 1) * P],
                                             rows(i, t)[:, k * P:(k + 1) * P], ident[:, :])
                        m.then_inc(S("n_ht"), 1)

                norm_transposes(0, range(TILES), lambda i, t: hrow[:, i % 2, :])
                pe.wait_ge(S("n_hT"), nb_(0, L) + TILES)
                pe.wait_ge(S("small"), B("small", L) + 16 * 8)

                for t in range(TILES):
                    for k in range(KD):
                        m = pe.matmul(ps[:, 7, t * 32:(t + 1) * 32], hT[:, k, t * P:(t + 1) * P], wkr[:, k, :],
                                      start=(k == 0), stop=(k == KD - 1))
                m.then_inc(S("kr"), 1)
                rows_chunk(L, range(TILES), S("c0"))
                pe.wait_ge(S("kre"), B("kre", L) + 1)
                for t in range(TILES):
                    pe.wait_ge(S("c0r"), B("c0r", L) + t + 1)
                    if t >= CT:
                        pe.wait_ge(S("rope"), B("rope", L) + t - CT + 1)
                    if t >= 2:
                        pe.wait_ge(S("qe"), B("qe", L) + t - 1)
                    for h in range(HEADS):
                        m = pe.transpose(ps[0:MLA_QK, 6 + t % 2, h * P:(h + 1) * P],
                                         prow[:, t % 3, h * MLA_QK:(h + 1) * MLA_QK], ident[:, :])
                    m.then_inc(S("qt"), 1)
                pe.wait_ge(S("qe"), B("qe", L) + TILES)
                pe.wait_ge(S("krr"), B("krr", L) + 1)
                for t in range(TILES):
                    m = pe.transpose(ps[0:MLA_QK, 6 + t // 4, (t % 4) * P:(t % 4 + 1) * P], krrow[:, t, :], ident[:, :])
                m.then_inc(S("krt"), 1)
                pe.wait_ge(S("ckn"), B("ckn", L) + TILES)
                for t in range(TILES):
                    m = pe.transpose(ps[:, 4 + t // 4, (t % 4) * P:(t % 4 + 1) * P], ckv[:, t, :], ident[:, :])
                m.then_inc(S("ckt"), 1)
                pe.wait_ge(S("cke"), B("cke", L) + 1)
                for h in range(HEADS):
                    if h >= 2:
                        pe.wait_ge(S("kne"), B("kne", L) + h - 1)
                    b = 2 * (h % 2)
                    pe.matmul(ps[0:HD, b, :], wukv[:, h * P:h * P + HD], ckvT[:, 0:512], start=True, stop=True)
                    pe.matmul(ps[0:HD, b + 1, 0:256], wukv[:, h * P:h * P + HD], ckvT[:, 512:768],
                              start=True, stop=True).then_inc(S("kn"), 1)
                wv = wukv[:, :].rearrange("p (h e) -> p h e", e=P)[:, :, HD:P]
                for t in range(TILES):
                    if t >= 2:
                        pe.wait_ge(S("vme"), B("vme", L) + t - 1)
                    pe.matmul(ps[:, 4 + t % 2, 0:GW], ckvT[:, t * P:(t + 1) * P], wv,
                              start=True, stop=True).then_inc(S("vmm"), 1)
                pe.wait_ge(S("vme"), B("vme", L) + TILES)
                pe.wait_ge(S("kne"), B("kne", L) + HEADS)
                pe.wait_ge(S("kte"), B("kte", L) + 1)
                rows_chunk(L, range(TILES), S("c1"))
                for t in range(TILES):
                    pe.wait_ge(S("c1r"), B("c1r", L) + t + 1)
                    if t >= CT:
                        pe.wait_ge(S("rop2"), B("rop2", L) + t - CT + 1)
                    if t >= 2:
                        pe.wait_ge(S("sqe"), B("sqe", L) + t - 1)
                    for b in range(2):
                        pe.transpose(ps[:, 6 + t % 2, b * P:(b + 1) * P],
                                     prow[:, t % 3, b * P:(b + 1) * P],
                                     ident[:, :])
                    pe.transpose(ps[:, 6 + t % 2, 2 * P:3 * P], prow[:, t % 3, GW:GW + P],
                                 ident[:, :]).then_inc(S("sqt"), 1)
                pe.wait_ge(S("sqe"), B("sqe", L) + TILES)

                def attention(kind):
                    ab = att_base(kind, L)
                    items = attention_items(kind, L)
                    N = len(items)
                    if kind == "mla":
                        pe.wait_ge(S("krc"), B("krc", L) + 1)

                    def ops(t, h):
                        if kind == "mla":
                            return qm[0:MLA_QK, h, :], km[0:MLA_QK, h, :]
                        r0 = HD * (h // 2) if kind == "swa" else HD * (h % 2)
                        b = h % 2 if kind == "swa" else h // 2
                        q, k = (sq, sk) if kind == "swa" else (nq, nk)
                        return q[r0:r0 + HD, b, :], k[r0:r0 + HD, 0 if kind == "swa" else b, :]

                    def scores(i):
                        t, h, spans = items[i]
                        if i >= 2:
                            pe.wait_ge(S("a_exp"), ab + i - 1)
                        q, k = ops(t, h)
                        q = q[:, t * P:(t + 1) * P]
                        at = 0
                        for first, w in spans:
                            done = 0
                            while done < w:
                                c = min(w - done, 512 - at % 512)
                                m = pe.matmul(ps[:, 2 * (i % 2) + at // 512, at % 512:at % 512 + c], q,
                                              k[:, first + done:first + done + c], start=True, stop=True)
                                done += c
                                at += c
                        m.then_inc(S("a_s"), 1)

                    def turn(i):
                        w = width(items[i][2])
                        pe.wait_ge(S("a_exp"), ab + i + 1)
                        if i >= 1:
                            pe.wait_ge(S("a_pt"), ab + i)
                        for b in range(w // P):
                            m = pe.transpose(ps[:, 4 + b // 4, (b % 4) * P:(b % 4 + 1) * P],
                                             pr[:, i % 2, b * P:(b + 1) * P], ident[:, :])
                        m.then_inc(S("a_t"), 1)

                    def values(i):
                        t, h, spans = items[i]
                        pe.wait_ge(S("a_pt"), ab + i + 1)
                        if i >= 2:
                            pe.wait_ge(S("a_y"), ab + i - 1)
                        if i % HEADS == 1 and i > HEADS:
                            pe.wait_ge(S("a_ye"), ab // HEADS + i // HEADS)
                        rows = []
                        for first, w in spans:
                            if kind == "na" and first:
                                strip = CT + (first - NCTX) // HD
                                rows += [vn[:, strip, h * HD:(h + 1) * HD], vn[:, strip + 2, h * HD:(h + 1) * HD]]
                                continue
                            for tt in range(first // P, (first + w) // P):
                                if kind == "mla":
                                    rows.append(vm[:, tt, h * HD:(h + 1) * HD])
                                elif kind == "swa":
                                    rows.append(vs[:, tt, (h // 2) * HD:(h // 2 + 1) * HD])
                                else:
                                    rows.append(vn[:, tt, h * HD:(h + 1) * HD])
                        for b, v in enumerate(rows):
                            m = pe.matmul(ps[:, 6 + i % 2, 0:HD], pT[:, i % 2, b * P:(b + 1) * P], v,
                                          start=(b == 0), stop=(b == len(rows) - 1))
                        m.then_inc(S("a_o"), 1)

                    def turn_y(j):
                        pe.wait_ge(S("a_y"), ab + HEADS * (j + 1))
                        for b in range(2):
                            m = pe.transpose(ps[:, 7, b * P:(b + 1) * P], yr[:, j % 2, b * P:(b + 1) * P], ident[:, :])
                        m.then_inc(S("a_yt"), 1)

                    for i in range(N + 3):
                        if i < N:
                            scores(i)
                        if 1 <= i <= N:
                            turn(i - 1)
                        if 2 <= i <= N + 1:
                            values(i - 2)
                        if i >= 6 and i % HEADS == 2:
                            turn_y(i // HEADS - 1)
                    pe.wait_ge(S("a_ye"), ab // HEADS + N // HEADS)

                attention("mla")
                attention("swa")
                g = take(2)
                for b in range(4):
                    for k in range(KD):
                        pe.matmul(ps[:, b, :], wsl(g, k, b * P, (b + 1) * P), hT[:, k, NCTX:TOK], start=(k == 0), stop=(k == KD - 1))
                    for k in range(KD):
                        m = pe.matmul(ps[:, 4 + b, 0:NCTX], wsl(g, k, b * P, (b + 1) * P),
                                      hT[:, k, 0:NCTX], start=(k == 0), stop=(k == KD - 1))
                    m.then_inc(S("c2"), 1)
                g = take(2)
                pe.wait_ge(S("c2e"), B("c2e", L) + 4)
                for b in range(4):
                    for k in range(KD):
                        pe.matmul(ps[:, b, :], wsl(g, k, b * P, (b + 1) * P), hT[:, k, NCTX:TOK], start=(k == 0), stop=(k == KD - 1))
                    for k in range(KD):
                        m = pe.matmul(ps[:, 4 + b, 0:NCTX], wsl(g, k, b * P, (b + 1) * P),
                                      hT[:, k, 0:NCTX], start=(k == 0), stop=(k == KD - 1))
                    m.then_inc(S("c3"), 1)
                pe.wait_ge(S("c3e"), B("c3e", L) + 4)
                for v in range(9):
                    if v >= 2:
                        pe.wait_ge(S("vne"), B("vne", L) + v - 1)
                    first = v * P if v < CT else NCTX + HD * (v - CT)
                    for b in range(2):
                        m = pe.transpose(ps[:, 6 + v % 2, b * P:(b + 1) * P], pr[:, b, first:first + P], ident[:, :])
                    m.then_inc(S("vnt"), 1)
                pe.wait_ge(S("vne"), B("vne", L) + 9)
                attention("na")
                rows_chunk(L, range(TILES), S("c4"))
                pe.wait_ge(S("c4e"), B("c4e", L) + TILES)
                for t in range(TILES):
                    if t >= 2:
                        pe.wait_ge(S("rke"), B("rke", L) + t - 1)
                    for b in range(2):
                        m = pe.transpose(ps[:, 6 + t % 2, b * P:(b + 1) * P], rkr[:, t, b * P:(b + 1) * P], ident[:, :])
                    m.then_inc(S("rkt"), 1)
                rows_chunk(L, range(TILES), S("c5"))
                pe.wait_ge(S("rke"), B("rke", L) + TILES)
                pe.wait_ge(S("c5e"), B("c5e", L) + TILES)
                for t in range(TILES):
                    pe.wait_ge(S("kd"), B("kd", L) + t + 1)
                    for b in range(2):
                        for d in range(2):
                            m = pe.matmul(ps[:, t, (2 * b + d) * P:(2 * b + d + 1) * P], kd[:, t % 2, d, b * P:(b + 1) * P],
                                          rv[:, t, b * P:(b + 1) * P], start=True, stop=True)
                    m.then_inc(S("u"), 1)
                pe.wait_ge(S("st"), B("st", L) + 1)
                pe.wait_ge(S("qd"), B("qd", L) + 4)
                tiles = list(range(lo, TILES))
                for i in range(len(tiles) + 2):
                    if i < len(tiles):
                        t = tiles[i]
                        if i >= 2:
                            pe.wait_ge(S("pfb"), B("pfb", L) + i - 1)
                        for h in range(HEADS):
                            r0 = HD * (h % 2)
                            m = pe.matmul(ps[:, 2 * (i % 2) + h % 2, (h // 2) * P:(h // 2 + 1) * P], rk[r0:r0 + HD, h // 2, t * P:(t + 1) * P],
                                          rq[r0:r0 + HD, h // 2, t * P:(t + 1) * P], start=True, stop=True)
                        m.then_inc(S("inner"), 1)
                    if 1 <= i <= len(tiles):
                        t, j = tiles[i - 1], i - 1
                        pe.wait_ge(S("pfb"), B("pfb", L) + j + 1)
                        if j >= 2:
                            pe.wait_ge(S("oc"), B("oc", L) + j - 1)
                        for d in range(2):
                            for b in range(2):
                                o = ps[:, 4 + j % 2, d * GW + b * P:d * GW + (b + 1) * P]
                                pe.matmul(o, qd[:, b, d, t * P:(t + 1) * P], st[:, t, 2 * b + d, :], start=True, stop=False,
                                          skip_group_check=True)
                                for h in (2 * b, 2 * b + 1):
                                    m = pe.matmul(ps[:, 4 + j % 2, d * GW + h * HD:d * GW + (h + 1) * HD],
                                                  pfb[:, j % 2, d, h * P:(h + 1) * P], rv[:, t, h * HD:(h + 1) * HD],
                                                  start=False, stop=True, skip_group_check=True)
                        m.then_inc(S("ro"), 1)
                    if i >= 2:
                        j = i - 2
                        pe.wait_ge(S("ry"), B("ry", L) + j + 1)
                        if j >= 2:
                            pe.wait_ge(S("rye"), B("rye", L) + j - 1)
                        for b in range(2):
                            m = pe.transpose(ps[:, 6 + j % 2, b * P:(b + 1) * P], on[:, j % 2, b * P:(b + 1) * P], ident[:, :])
                        m.then_inc(S("ryt"), 1)
                pe.wait_ge(S("rye"), B("rye", L) + len(tiles))
                hT_or_y[0] = yT
                for c in range(2):
                    if c:
                        pe.wait_ge(S("og"), B("og", L) + len(tiles))
                    rows_chunk(L, tiles, S("op"))
                hT_or_y[0] = hT
                pe.wait_ge(S("og"), B("og", L) + 2 * len(tiles))
                norm_transposes(1, tiles, lambda i, t: h2[:, t, :])
                pe.wait_ge(S("n_hT"), nb_(1, L) + len(tiles))
                for j in range(2 * PH):
                    if j % 4 == 0:
                        g = take(2)
                    if j >= 2:
                        pe.wait_ge(S("fqe"), B("fqe", L) + j - 1)
                    c0 = (j % 4) * P
                    for k in range(KD):
                        m = pe.matmul(ps[:, 2 * (j % 2), :], wsl(g, k, c0, c0 + P), hT[:, k, NCTX:TOK], start=(k == 0), stop=(k == KD - 1))
                    if lo == 0:
                        for k in range(KD):
                            m = pe.matmul(ps[:, 2 * (j % 2) + 1, 0:256], wsl(g, k, c0, c0 + P), hT[:, k, 0:NCTX],
                                          start=(k == 0), stop=(k == KD - 1))
                    m.then_inc(S("fq"), 1)
                    if j >= 1:
                        key_scores = j - 1
                        pe.wait_ge(S("fqe"), B("fqe", L) + key_scores + 1)
                        if key_scores >= 2:
                            pe.wait_ge(S("fse"), B("fse", L) + key_scores - 1)
                        for t in tiles:
                            m = pe.matmul(ps[:, 4 + 2 * (key_scores % 2) + t // 4, (t % 4) * P:(t % 4 + 1) * P],
                                          qTb[:, key_scores % 2, t * P:(t + 1) * P], keysT[:, key_scores % 2, :], start=True, stop=True)
                        m.then_inc(S("fs"), 1)
                j = 2 * PH - 1
                pe.wait_ge(S("fqe"), B("fqe", L) + j + 1)
                pe.wait_ge(S("fse"), B("fse", L) + j - 1)
                for t in tiles:
                    m = pe.matmul(ps[:, 4 + 2 * (j % 2) + t // 4, (t % 4) * P:(t % 4 + 1) * P],
                                  qTb[:, j % 2, t * P:(t + 1) * P], keysT[:, j % 2, :], start=True, stop=True)
                m.then_inc(S("fs"), 1)
                pe.wait_ge(S("fse"), B("fse", L) + 2 * PH)
                with pe.Fori(0, len(tiles)) as i:
                    pe.wait_ge(S("stg"), B("stg", L) + i + 1)
                    for s in range(SLOTS):
                        pe.wait_ge(S("dg"), B("dg", L) + SLOTS * i + s + 1)
                        for h in range(2):
                            m = pe.matmul(ps[:, h, :], dg[:, s % 8, :], uvr[:, s % UVRING, D + 512 * h:D + 512 * h + 512],
                                          start=(s == 0), stop=(s == SLOTS - 1))
                        m.then_inc(S("em"), 1)

        @block.scalar
        def _(act):
            link = Chain(act, S("act"))
            act.wait_ge(S("in"), 16 * 9)
            nc.scalar.activation(cE[:, :, :], cT[:, :, :], ACT.Exp, scale=-1.0).then_inc(S("ce"), 1)
            for L in range(LAYERS):
                n = f"_{L}"
                lo = first_out[L]
                tiles = list(range(lo, TILES))
                if L:
                    act.wait_ge(S("layer"), L)
                for c in range(ADA_CHUNKS):
                    if c == 0:
                        for q in range(2):
                            act.dma_start(adab[0:2, q, :], a["ada_b"][L:L + 1, q * CH:(q + 1) * CH].partition_broadcast(2).rearrange("a b c -> a (b c)")).then_inc(S(f"ab{q}"), 16)
                    act.wait_ge(S("mrow"), B("mrow", L) + c + 1)
                    act.dma_start(mods[L, :, c * CH:(c + 1) * CH], mrow[0:2, c % 2, :]).then_inc(S(f"ms{c % 2}"), 16)
                    if c + 2 < ADA_CHUNKS:
                        act.dma_start(adab[0:2, c % 2, :], a["ada_b"][L:L + 1, (c + 2) * CH:(c + 3) * CH].partition_broadcast(2).rearrange("a b c -> a (b c)")).then_inc(S(f"ab{c % 2}"), 16)

                def norm(tag, tiles, part, rows):
                    for q in range(2):
                        act.wait_ge(S(f"ms{q}"), B(f"ms{q}", L) + 16 * (ADA_CHUNKS // 2))
                    for s in range(2):
                        for w, c in ((0, part + 1), (1, part)):
                            act.dma_start(tabs[:, 2 * s + w, :], mods[L, s:s + 1, c * D:(c + 1) * D].partition_broadcast(P).rearrange("a b c -> a (b c)")).then_inc(S("n_tab"), 16)
                    g = a["norm_mix_g"] if part == 0 else a["norm_ffn_g"]
                    act.dma_start(gbc, g[L:L + 1, :].partition_broadcast(P).rearrange("a b c -> a (b c)")).then_inc(S("n_tab"), 16)
                    for i, t in enumerate(tiles):
                        if i:
                            act.wait_ge(S("n_sq"), nb_(tag, L) + i)
                        nc.scalar.activation(junk, xs[:, t, :], ACT.Square, accum_out=stat[:, 0, t:t + 1]).then_inc(S("n_sq"), 1)
                    act.wait_ge(S("n_sq"), nb_(tag, L) + len(tiles))
                    act.wait_ge(S("eps"), 1)
                    t0 = tiles[0]
                    nc.scalar.activation(stat[:, 1, t0:TILES], stat[:, 0, t0:TILES], ACT.Sqrt, scale=1.0 / D, bias=eps[:, 0:1]).then_inc(S("n_rt"), 1)
                    for i, t in enumerate(tiles):
                        act.wait_ge(S("n_ht"), nb_(tag, L) + i + 1)
                        b = 2 * (i % 2)
                        nc.scalar.activation(hT[:, :, t * P:(t + 1) * P],
                                             ps[:, b:b + 2, :].rearrange("p a (k q) -> p (a k) q", q=P), ACT.Copy).then_inc(S("n_hT"), 1)

                norm(0, range(TILES), 0, None)
                act.wait_ge(S("kr"), B("kr", L) + 1)
                act.wait_ge(S("krz"), B("krz", L) + 1)
                nc.scalar.activation(krrow[:, :, HD:MLA_QK], ps[:, 7, 0:6 * 32].rearrange("p (t q) -> p t q", q=32), ACT.Copy).then_inc(S("kre"), 1)

                def q_out(t):
                    act.wait_ge(S("qt"), B("qt", L) + t + 1)
                    nc.scalar.activation(qm[0:MLA_QK, :, t * P:(t + 1) * P],
                                         ps[0:MLA_QK, 6 + t % 2, :].rearrange("p (h q) -> p h q", q=P), ACT.Copy).then_inc(S("qe"), 1)

                for t in range(TILES):
                    act.wait_ge(S("c0"), B("c0", L) + t + 1)
                    if t >= 3:
                        act.wait_ge(S("qt"), B("qt", L) + t - 2)
                    nc.scalar.activation(ckv[:, t, :], ps[:, t, 384:512], ACT.Copy).then_inc(S("ckr"), 1)
                    nc.scalar.activation(prow[:, t % 3, 0:384], ps[:, t, 0:384], ACT.Copy).then_inc(S("c0r"), 1)
                    if t:
                        q_out(t - 1)
                q_out(TILES - 1)
                act.wait_ge(S("krt"), B("krt", L) + 1)
                nc.scalar.activation(km[HD:MLA_QK, 0, :], ps[HD:MLA_QK, 6:8, :].rearrange("p a b -> p (a b)")[:, 0:TOK], ACT.Copy).then_inc(S("kte"), 1)
                act.wait_ge(S("cks"), B("cks", L) + TILES)
                nc.scalar.activation(stat[:, 1, 0:TILES], stat[:, 0, 0:TILES], ACT.Sqrt, scale=1.0 / P, bias=eps[:, 0:1]).then_inc(S("ckq"), 1)
                act.wait_ge(S("ckt"), B("ckt", L) + 1)
                nc.scalar.activation(ckvT, ps[:, 4:6, :].rearrange("p a b -> p (a b)")[:, 0:TOK], ACT.Copy).then_inc(S("cke"), 1)
                for h in range(HEADS):
                    act.wait_ge(S("kn"), B("kn", L) + h + 1)
                    b = 2 * (h % 2)
                    nc.scalar.activation(km[0:HD, h, :], ps[0:HD, b:b + 2, :].rearrange("p a b -> p (a b)")[:, 0:TOK], ACT.Copy).then_inc(S("kne"), 1)

                def sq_out(t):
                    act.wait_ge(S("sqt"), B("sqt", L) + t + 1)
                    nc.scalar.activation(sq[:, :, t * P:(t + 1) * P], ps[:, 6 + t % 2, 0:2 * P].rearrange("p (b q) -> p b q", q=P), ACT.Copy, scale=0.125)
                    nc.scalar.activation(sk[:, 0, t * P:(t + 1) * P], ps[:, 6 + t % 2, 2 * P:3 * P], ACT.Copy).then_inc(S("sqe"), 1)

                for t in range(TILES):
                    act.wait_ge(S("c1"), B("c1", L) + t + 1)
                    if t >= 3:
                        act.wait_ge(S("sqt"), B("sqt", L) + t - 2)
                    else:
                        act.wait_ge(S("qt"), B("qt", L) + TILES)
                    nc.scalar.activation(vs[:, t, :], ps[:, t, 384:512], ACT.Copy)
                    nc.scalar.activation(prow[:, t % 3, 0:GW].rearrange("p (r g d) -> p g r d", g=2, r=2),
                                         ps[:, t, 0:GW].rearrange("p (g r d) -> p g r d", g=2, r=2), ACT.Copy)
                    nc.scalar.activation(prow[:, t % 3, GW:384], ps[:, t, GW:384], ACT.Copy).then_inc(S("c1r"), 1)
                    if t:
                        sq_out(t - 1)
                sq_out(TILES - 1)

                def attention(kind):
                    ab = att_base(kind, L)
                    items = attention_items(kind, L)
                    N = len(items)

                    def y_out(j):
                        act.wait_ge(S("a_yt"), ab // HEADS + j + 1)
                        t = items[HEADS * j][0]
                        kb = {"mla": 0, "swa": 2, "na": 4}[kind]
                        for b in range(2):
                            src = ps[:, 7, b * P:(b + 1) * P]
                            if kind == "na" and t >= CT:
                                s0 = 2 * (t - CT)
                                dst = yT[:, kb + b, NCTX:TOK].rearrange("p (r s c) -> p s r c", r=ROWS, c=8)[:, s0:s0 + 2]
                                src = src.rearrange("p (s r c) -> p s r c", s=2, c=8)
                            else:
                                dst = yT[:, kb + b, t * P:(t + 1) * P]
                            m = nc.scalar.activation(dst, src, ACT.Copy, scale=beta[:, kb + b:kb + b + 1])
                        m.then_inc(S("a_ye"), 1)

                    for i in range(N + 3):
                        if i < N:
                            w = width(items[i][2])
                            act.wait_ge(S("a_nm"), ab + i + 1)
                            if i >= 2:
                                act.wait_ge(S("a_t"), ab + i - 1)
                            c = i % 32
                            if kind == "swa":
                                nc.scalar.activation(att[:, 3, c:c + 1], smallw[:, items[i][1]:items[i][1] + 1], ACT.Exp, bias=att[:, 1, c:c + 1])
                            nc.scalar.activation(pr[:, i % 2, 0:w], ps[:, 2 * (i % 2):2 * (i % 2) + 2, :].rearrange("p a b -> p (a b)")[:, 0:w],
                                                 ACT.Exp, scale=MLA_SCALE if kind == "mla" else 1.0,
                                                 bias=att[:, 1, c:c + 1], accum_out=att[:, 2, c:c + 1]).then_inc(S("a_exp"), 1)
                        if i >= 6 and i % HEADS == 2:
                            y_out(i // HEADS - 1)

                attention("mla")
                attention("swa")
                def by_strip(x):
                    return x.rearrange("p (s r c) -> p r s c", r=ROWS, c=8)

                for b in range(4):
                    act.wait_ge(S("c2"), B("c2", L) + b + 1)
                    dst, s = (nq, 0.125) if b < 2 else (nk, 1.0)
                    nc.scalar.activation(by_strip(dst[:, b % 2, NCTX:TOK]), ps[:, b, :].rearrange("p (r s c) -> p r s c", r=ROWS, c=8), ACT.Copy, scale=s)
                    nc.scalar.activation(dst[:, b % 2, 0:NCTX], ps[:, 4 + b, 0:NCTX], ACT.Copy, scale=s).then_inc(S("c2e"), 1)
                for b in range(4):
                    act.wait_ge(S("c3"), B("c3", L) + b + 1)
                    if b < 2:
                        nc.scalar.activation(by_strip(pr[:, b, NCTX:TOK]), ps[:, b, :].rearrange("p (r s c) -> p r s c", r=ROWS, c=8), ACT.Copy)
                        nc.scalar.activation(pr[:, b, 0:NCTX], ps[:, 4 + b, 0:NCTX], ACT.Copy).then_inc(S("c3e"), 1)
                    else:
                        nc.scalar.activation(rq[:, b - 2, NCTX:TOK], ps[:, b, :], ACT.Copy)
                        nc.scalar.activation(rq[:, b - 2, 0:NCTX], ps[:, 4 + b, 0:NCTX], ACT.Copy).then_inc(S("c3e"), 1)
                for v in range(9):
                    act.wait_ge(S("vnt"), B("vnt", L) + v + 1)
                    nc.scalar.activation(vn[:, v, :], ps[:, 6 + v % 2, 0:GW], ACT.Copy).then_inc(S("vne"), 1)
                attention("na")
                for t in range(TILES):
                    act.wait_ge(S("c4"), B("c4", L) + t + 1)
                    nc.scalar.activation(rkr[:, t, :], ps[:, t, 0:GW], ACT.Copy, scale=0.125)
                    nc.scalar.activation(rv[:, t, :], ps[:, t, GW:2 * GW], ACT.Copy).then_inc(S("c4e"), 1)
                dec = smallw[:, 4:16]
                act.wait_ge(S("dabs"), B("dabs", L) + 1)
                nc.scalar.activation(rsm[:, 12:24], rsm[:, 0:12], ACT.Exp, scale=-1.0).then_inc(S("dex"), 1)
                act.wait_ge(S("dex"), B("dex", L) + 1)
                nc.scalar.activation(rsm[:, 24:36], rsm[:, 12:24], ACT.Ln, bias=1.0).then_inc(S("dln"), 1)
                act.wait_ge(S("lg"), B("lg", L) + 1)
                nc.scalar.activation(rsm[:, 56:64], rsm[:, 48:56], ACT.Exp).then_inc(S("kd8"), 1)
                nc.scalar.activation(rsm[:, 0:4], rsm[:, 44:48], ACT.Exp, scale=float(P)).then_inc(S("cd"), 1)
                act.wait_ge(S("rtab"), B("rtab", L) + 32)
                for d in range(2):
                    for h in range(HEADS):
                        c = 36 + 4 * d + h
                        nc.scalar.activation(dt_[:, d, h, :], rtab[:, d, :], ACT.Exp, scale=rsm[:, c:c + 1]).then_inc(S("dt"), 1)
                for b in range(2):
                    for d in range(2):
                        c = 44 + 2 * b + d
                        nc.scalar.activation(qdt[:, b, d, :], ptab[:, d * P:(d + 1) * P], ACT.Exp, scale=rsm[:, c:c + 1]).then_inc(S("qdt"), 1)
                for t in range(TILES):
                    act.wait_ge(S("rkt"), B("rkt", L) + t + 1)
                    nc.scalar.activation(rk[:, :, t * P:(t + 1) * P], ps[:, 6 + t % 2, 0:2 * P].rearrange("p (b q) -> p b q", q=P), ACT.Copy).then_inc(S("rke"), 1)
                for t in range(TILES):
                    act.wait_ge(S("c5"), B("c5", L) + t + 1)
                    if t >= 2:
                        act.wait_ge(S("c5d"), B("c5d", L) + t - 1)
                    nc.scalar.activation(gate[:, t, :], ps[:, t, :], ACT.Copy)
                    nc.scalar.activation(on[:, t % 2, :], ps[:, t, :], ACT.Exp, scale=-1.0).then_inc(S("c5e"), 1)
                for j, t in enumerate(tiles):
                    act.wait_ge(S("gv"), B("gv", L) + j + 1)
                    nc.scalar.activation(rsm[:, 20:28], rsm[:, 12:20], ACT.Sqrt, scale=1.0 / HD, bias=eps[:, 0:1]).then_inc(S("gr"), 1)
                    act.wait_ge(S("ryt"), B("ryt", L) + j + 1)
                    for b in range(2):
                        m = nc.scalar.activation(yT[:, 6 + b, t * P:(t + 1) * P], ps[:, 6 + j % 2, b * P:(b + 1) * P], ACT.Copy, scale=beta[:, 6 + b:7 + b])
                    m.then_inc(S("rye"), 1)
                for s in range(2):
                    act.dma_start(tabs[:, s, :], mods[L, s:s + 1, 2 * D:3 * D].partition_broadcast(P).rearrange("a b c -> a (b c)")).then_inc(S("gt"), 16)
                act.wait_ge(S("xo"), B("xo", L) + 2 * len(tiles))
                norm(1, tiles, 3, None)
                def store_scores(j):
                    act.wait_ge(S("fse"), B("fse", L) + j + 1)
                    act.dma_start(scores_d[lo:TILES, :, j, :].rearrange("t p n -> p t n"),
                                  stage[:, j % 2, lo * P:TOK].rearrange("p (t n) -> p t n", n=NKEYS)).then_inc(S(f"sd{j % 2}"), 16)

                for j in range(2 * PH):
                    if j >= 2:
                        store_scores(j - 2)
                    act.wait_ge(S("fq"), B("fq", L) + j + 1)
                    if j >= 2:
                        act.wait_ge(S("fs"), B("fs", L) + j - 1)
                    if lo == 0:
                        nc.scalar.activation(qTb[:, j % 2, 0:NCTX], ps[:, 2 * (j % 2) + 1, 0:256], ACT.Copy)
                    nc.scalar.activation(qTb[:, j % 2, NCTX:TOK], ps[:, 2 * (j % 2), :], ACT.Copy).then_inc(S("fqe"), 1)
                store_scores(2 * PH - 2)
                store_scores(2 * PH - 1)
                for s in range(2):
                    act.dma_start(gtab[:, s, :], mods[L, s:s + 1, 5 * D:6 * D].partition_broadcast(P).rearrange("a b c -> a (b c)")).then_inc(S("gt2"), 16)
                act.wait_ge(S("gx"), B("gx", L) + 1)
                nc.scalar.activation(gx[:, 1, :], gx[:, 0, :], ACT.Exp).then_inc(S("ge"), 1)

                def expert_gelus(i, ahead):
                    for q in range(SLOTS // BATCH):
                        act.wait_ge(S("dot"), B("dot", L) + (SLOTS // BATCH) * i + q + 1)
                        nc.scalar.activation(agel[:, q * BATCH:(q + 1) * BATCH], adot[:, q * BATCH:(q + 1) * BATCH], ACT.Gelu).then_inc(S("gel"), 1)
                        if ahead and q == GATES_AT:
                            act.wait_ge(S("gx"), B("gx", L) + i + 2)
                            nc.scalar.activation(gx[:, 1, :], gx[:, 0, :], ACT.Exp).then_inc(S("ge"), 1)

                with act.Fori(0, len(tiles) - 1) as i:
                    expert_gelus(i, True)
                expert_gelus(len(tiles) - 1, False)
            for i, t in enumerate(tiles):
                act.wait_ge(S("layer"), LAYERS)
                nc.scalar.activation(gjunk, xs[:, t, :], ACT.Square, accum_out=stat[:, 0, t:t + 1]).then_inc(S("fsq"), 1)
                act.wait_ge(S("fsq"), i + 1)
            nc.scalar.activation(stat[:, 1, CT:TILES], stat[:, 0, CT:TILES], ACT.Sqrt, scale=1.0 / D, bias=eps[:, 0:1]).then_inc(S("frt"), 1)

        @block.vector
        def _(v):
            link = Chain(v, S("dve"))
            link.own = S("max_steps")
            v.memset(eps[:, :], EPS).then_inc(S("eps"), 1)
            v.wait_ge(S("ce"), 1)
            link(v.tensor_scalar(cE[:, :, :], cE[:, :, :], 1.0, None, ALU.add))
            link(v.reciprocal(cE[:, :, :], cE[:, :, :]))
            v.tensor_tensor(cT[:, :, :], cT[:, :, :], cE[:, :, :], ALU.mult).then_inc(S("silu"), 1)
            for L in range(LAYERS):
                n = f"_{L}"
                lo = first_out[L]
                tiles = list(range(lo, TILES))
                for c in range(ADA_CHUNKS):
                    v.wait_ge(S("mps"), B("mps", L) + c + 1)
                    v.wait_ge(S(f"ab{c % 2}"), B(f"ab{c % 2}", L) + 16 * (c // 2 + 1))
                    if c >= 2:
                        v.wait_ge(S(f"ms{c % 2}"), B(f"ms{c % 2}", L) + 16 * (c // 2))
                    v.tensor_tensor(mrow[0:2, c % 2, :], ps[0:2, c % 2, :], adab[0:2, c % 2, :], ALU.add).then_inc(S("mrow"), 1)

                def norm(tag, tiles, rows, free):
                    v.wait_ge(S("n_tab"), 16 * 5 * (2 * L + tag + 1))
                    for s in range(2):
                        link(v.scalar_tensor_tensor(tabs[:, 2 * s, :], tabs[:, 2 * s, :], 1.0, gbc, ALU.add, ALU.mult))
                    v.wait_ge(S("n_rt"), 2 * L + tag + 1)
                    t0 = tiles[0]
                    link(v.reciprocal(stat[:, 2, t0:TILES], stat[:, 1, t0:TILES]))
                    for i, t in enumerate(tiles):
                        s = 0 if t < CT else 1
                        r = rows(i, t)
                        if free and i >= 2:
                            v.wait_ge(S("n_ht"), nb_(tag, L) + i - 1)
                        link(v.scalar_tensor_tensor(r, xs[:, t, :], stat[:, 2, t:t + 1], tabs[:, 2 * s, :], ALU.mult, ALU.mult))
                        v.tensor_tensor(r, r, tabs[:, 2 * s + 1, :], ALU.add).then_inc(S("n_h"), 1)

                norm(0, range(TILES), lambda i, t: hrow[:, i % 2, :], True)

                def rope(x1, x2, cos, sin, tmp):
                    v.tensor_tensor(tmp[0], x1, cos, ALU.mult)
                    v.tensor_tensor(tmp[1], x2, sin, ALU.mult)
                    v.tensor_tensor(tmp[2], x1, sin, ALU.mult)
                    link(v.tensor_tensor(tmp[3], x2, cos, ALU.mult))
                    v.tensor_tensor(x1, tmp[0], tmp[1], ALU.subtract)
                    return v.tensor_tensor(x2, tmp[2], tmp[3], ALU.add)

                v.wait_ge(S("n_hT"), nb_(0, L) + TILES)
                v.memset(krrow, 0.0).then_inc(S("krz"), 1)
                v.wait_ge(S("kre"), B("kre", L) + 1)
                kk = krrow[:, CT:TILES, HD:MLA_QK].rearrange("p t (x r q) -> p t x r q", x=2, r=2)
                tmp = pr[:, 0, 0:256].rearrange("p (i t x q) -> p i t x q", i=4, t=4, x=2)
                rope(kk[:, :, :, 0, :], kk[:, :, :, 1, :], rope16[:, :, 0, :, :], rope16[:, :, 1, :, :],
                     [tmp[:, i] for i in range(4)]).then_inc(S("krr"), 1)
                for t in range(TILES):
                    v.wait_ge(S("ckr"), B("ckr", L) + t + 1)
                    v.tensor_tensor_reduce(pT[:, 0, 0:P], ckv[:, t, :], ckv[:, t, :], 1.0, 0.0, ALU.mult, ALU.add, stat[:, 0, t:t + 1]).then_inc(S("cks"), 1)
                    v.wait_ge(S("cks"), B("cks", L) + t + 1)
                    if t >= CT:
                        v.wait_ge(S("c0r"), B("c0r", L) + t + 1)
                        xq = prow[:, t % 3, 0:384].rearrange("p (h q) -> p h q", q=MLA_QK)[:, :, HD:MLA_QK].rearrange("p h (x r q) -> p h x r q", x=2, r=2)
                        bc = [rope16[:, t - CT, w, :, :].unsqueeze(1).to_broadcast([P, HEADS, 2, 8]) for w in range(2)]
                        tmp = pr[:, 0, 0:256].rearrange("p (i t x q) -> p i t x q", i=4, t=4, x=2)
                        rope(xq[:, :, :, 0, :], xq[:, :, :, 1, :], bc[0], bc[1], [tmp[:, i] for i in range(4)]).then_inc(S("rope"), 1)
                        v.wait_ge(S("rope"), B("rope", L) + t - CT + 1)
                v.wait_ge(S("ckq"), B("ckq", L) + 1)
                v.wait_ge(S("small"), B("small", L) + 16 * 8)
                link(v.reciprocal(stat[:, 2, 0:TILES], stat[:, 1, 0:TILES]))
                for t in range(TILES):
                    v.scalar_tensor_tensor(ckv[:, t, :], ckv[:, t, :], stat[:, 2, t:t + 1], gkv[:, :], ALU.mult, ALU.mult).then_inc(S("ckn"), 1)
                for t in range(TILES):
                    v.wait_ge(S("vmm"), B("vmm", L) + t + 1)
                    v.tensor_copy(vm[:, t, :], ps[:, 4 + t % 2, 0:GW]).then_inc(S("vme"), 1)
                for t in range(CT, TILES):
                    v.wait_ge(S("c1r"), B("c1r", L) + t + 1)
                    xq = prow[:, t % 3, 0:384].rearrange("p (h x r q) -> p h x r q", h=6, x=2, r=2)
                    bc = [rope32[:, t - CT, w, :, :].unsqueeze(1).to_broadcast([P, 6, 2, 16]) for w in range(2)]
                    tmp = pr[:, 0, 0:768].rearrange("p (i t x q) -> p i t x q", i=4, t=6, x=2)
                    rope(xq[:, :, :, 0, :], xq[:, :, :, 1, :], bc[0], bc[1], [tmp[:, i] for i in range(4)]).then_inc(S("rop2"), 1)
                    v.wait_ge(S("rop2"), B("rop2", L) + t - CT + 1)

                def attention(kind):
                    ab = att_base(kind, L)
                    items = attention_items(kind, L)
                    N = len(items)
                    for i in range(N + 2):
                        if i < N:
                            t, h, spans = items[i]
                            w = width(spans)
                            c = i % 32
                            flat = ps[:, 2 * (i % 2):2 * (i % 2) + 2, :].rearrange("p a b -> p (a b)")
                            v.wait_ge(S("a_s"), ab + i + 1)
                            if kind == "swa" and t >= CT:
                                if t > CT:
                                    link(v.tensor_tensor(flat[:, 256:384], flat[:, 256:384], swam[:, 0, :], ALU.add))
                                if t < TILES - 1:
                                    link(v.tensor_tensor(flat[:, w - P:w], flat[:, w - P:w], swam[:, 1, :], ALU.add))
                            if kind == "na" and t >= CT:
                                j = i - (0 if lo else CT * HEADS)
                                v.wait_ge(S("nb"), B("nb", L) + j + 1)
                                link(v.tensor_tensor(flat[:, 256:512], flat[:, 256:512], nbias[:, j % 2, :], ALU.add))
                            link(v.reduce_max(att[:, 0, c:c + 1], flat[:, 0:w], AX))
                            if kind == "swa":
                                v.tensor_scalar(att[:, 1, c:c + 1], att[:, 0, c:c + 1], smallw[:, h:h + 1], -1.0, ALU.max, ALU.mult).then_inc(S("a_nm"), 1)
                            else:
                                v.tensor_scalar(att[:, 1, c:c + 1], att[:, 0, c:c + 1], -MLA_SCALE if kind == "mla" else -1.0, None, ALU.mult).then_inc(S("a_nm"), 1)
                        if 1 <= i <= N:
                            j = i - 1
                            w = width(items[j][2])
                            v.wait_ge(S("a_t"), ab + j + 1)
                            if j >= 2:
                                v.wait_ge(S("a_o"), ab + j - 1)
                            v.tensor_copy(pT[:, j % 2, 0:w], ps[:, 4:6, :].rearrange("p a b -> p (a b)")[:, 0:w]).then_inc(S("a_pt"), 1)
                        if i >= 2:
                            j = i - 2
                            c = j % 32
                            g = j // HEADS
                            h = items[j][1]
                            total = att[:, 2, c:c + 1]
                            if kind == "swa":
                                link(v.tensor_tensor(att[:, 4, c:c + 1], att[:, 2, c:c + 1], att[:, 3, c:c + 1], ALU.add))
                                total = att[:, 4, c:c + 1]
                            link(v.reciprocal(att[:, 5, c:c + 1], total))
                            v.wait_ge(S("a_o"), ab + j + 1)
                            if h == 0 and g >= 2:
                                v.wait_ge(S("a_yt"), ab // HEADS + g - 1)
                            v.tensor_scalar(yr[:, g % 2, h * HD:(h + 1) * HD], ps[:, 6 + j % 2, 0:HD],
                                            att[:, 5, c:c + 1], None, ALU.mult).then_inc(S("a_y"), 1)

                attention("mla")
                attention("swa")
                attention("na")
                link(v.tensor_scalar(rsm[:, 12:24], smallw[:, 4:16], -1.0, None, ALU.mult))
                v.tensor_tensor(rsm[:, 0:12], rsm[:, 12:24], smallw[:, 4:16], ALU.max).then_inc(S("dabs"), 1)
                v.wait_ge(S("dln"), B("dln", L) + 1)
                link(v.tensor_scalar(rsm[:, 0:12], smallw[:, 4:16], 0.0, None, ALU.min))
                link(v.tensor_tensor(rsm[:, 36:48], rsm[:, 0:12], rsm[:, 24:36], ALU.subtract))
                v.tensor_tensor(rsm[:, 48:56], rsm[:, 36:44], ptab[:, 2 * P:2 * P + 8], ALU.mult).then_inc(S("lg"), 1)
                for i in range(8):
                    d, h = i // 4, i % 4
                    v.wait_ge(S("dt"), B("dt", L) + i + 1)
                    v.tensor_tensor(dt_[:, d, h, :], dt_[:, d, h, :], rtab[:, 2 + d, :], ALU.mult).then_inc(S("dtm"), 1)
                for i in range(4):
                    b, d = i // 2, i % 2
                    v.wait_ge(S("qdt"), B("qdt", L) + i + 1)
                    v.tensor_tensor(qd[:, b, d, :].rearrange("p (t q) -> p t q", q=P), rq[:, b, :].rearrange("p (t q) -> p t q", q=P),
                                    qdt[:, b, d, :].unsqueeze(1).to_broadcast([P, TILES, P]), ALU.mult).then_inc(S("qd"), 1)
                v.wait_ge(S("kd8"), B("kd8", L) + 1)
                v.wait_ge(S("rtab"), B("rtab", L) + 32)
                v.wait_ge(S("c4e"), B("c4e", L) + TILES)
                for t in range(TILES):
                    v.wait_ge(S("c5e"), B("c5e", L) + t + 1)
                    link(v.tensor_scalar(on[:, t % 2, :], on[:, t % 2, :], 1.0, None, ALU.add))
                    link(v.reciprocal(on[:, t % 2, :], on[:, t % 2, :]))
                    link(v.tensor_tensor(gate[:, t, :], gate[:, t, :], on[:, t % 2, :], ALU.mult))
                    v.tensor_tensor(gate[:, t, :], gate[:, t, :], gn, ALU.mult).then_inc(S("c5d"), 1)
                for t in range(TILES):
                    if t >= 2:
                        v.wait_ge(S("u"), B("u", L) + t - 1)
                    for d in range(2):
                        m = v.tensor_tensor(kd[:, t % 2, d, :].rearrange("p (h e) -> p h e", e=HD), rkr[:, t, :].rearrange("p (h e) -> p h e", e=HD),
                                            rsm[:, 56 + 4 * d:60 + 4 * d].unsqueeze(2).to_broadcast([P, HEADS, HD]), ALU.mult)
                    m.then_inc(S("kd"), 1)
                v.wait_ge(S("u"), B("u", L) + TILES)
                v.wait_ge(S("cd"), B("cd", L) + 1)
                for d, order in ((0, [0, 1, 2, 3, 4, 5]), (1, [1, 0, 5, 4, 3, 2])):
                    for b in range(2):
                        last = v.memset(st[:, order[0], 2 * b + d, :], 0.0)
                link(last)
                for step in range(TILES - 1):
                    for d, order in ((0, [0, 1, 2, 3, 4, 5]), (1, [1, 0, 5, 4, 3, 2])):
                        for b in range(2):
                            c = 2 * b + d
                            last = v.scalar_tensor_tensor(st[:, order[step + 1], c, :], st[:, order[step], c, :], rsm[:, c:c + 1],
                                                          ps[:, order[step], c * P:(c + 1) * P], ALU.mult, ALU.add)
                    link(last)
                for t in range(TILES):
                    last = v.tensor_tensor(st[:, t, :, :], st[:, t, :, :], ptab[:, 2 * P + 8:3 * P + 8].unsqueeze(1).to_broadcast([P, 4, P]), ALU.mult)
                last.then_inc(S("st"), 1)
                v.wait_ge(S("dtm"), B("dtm", L) + 8)
                for j in range(len(tiles) + 1):
                    if j < len(tiles):
                        v.wait_ge(S("inner"), B("inner", L) + j + 1)
                        if j >= 2:
                            v.wait_ge(S("ro"), B("ro", L) + j - 1)
                        for d in range(2):
                            m = v.tensor_tensor(pfb[:, j % 2, d, :].rearrange("p (b w q) -> p b w q", b=2, w=2),
                                                ps[:, 2 * (j % 2):2 * (j % 2) + 2, 0:2 * P].rearrange("p w (b q) -> p b w q", b=2),
                                                dt_[:, d, :, :].rearrange("p (b w) q -> p b w q", w=2), ALU.mult)
                        m.then_inc(S("pfb"), 1)
                    if j >= 1:
                        q = j - 1
                        t = tiles[q]
                        v.wait_ge(S("ro"), B("ro", L) + q + 1)
                        if q >= 2:
                            v.wait_ge(S("ryt"), B("ryt", L) + q - 1)
                        o = on[:, q % 2, :].rearrange("p (g e) -> p g e", e=HD)
                        po = ps[:, 4 + q % 2, :].rearrange("p (g e) -> p g e", e=HD)
                        osg = osq.rearrange("p (g e) -> p g e", e=HD)
                        link(v.reduce_sum(rsm[:, 4:12], po, AX))
                        link(v.tensor_scalar(rsm[:, 4:12], rsm[:, 4:12], 1.0 / HD, None, ALU.mult))
                        v.tensor_tensor(o, po, rsm[:, 4:12].unsqueeze(2).to_broadcast([P, 8, HD]), ALU.subtract).then_inc(S("oc"), 1)
                        v.wait_ge(S("oc"), B("oc", L) + q + 1)
                        link(v.tensor_tensor(osg, o, o, ALU.mult))
                        v.reduce_sum(rsm[:, 12:20], osg, AX).then_inc(S("gv"), 1)
                        v.wait_ge(S("gr"), B("gr", L) + q + 1)
                        link(v.reciprocal(rsm[:, 28:36], rsm[:, 20:28]))
                        link(v.tensor_tensor(o, o, rsm[:, 28:36].unsqueeze(2).to_broadcast([P, 8, HD]), ALU.mult))
                        link(v.tensor_tensor(on[:, q % 2, :], on[:, q % 2, :], gate[:, t, :], ALU.mult))
                        v.tensor_tensor(on[:, q % 2, 0:GW], on[:, q % 2, 0:GW], on[:, q % 2, GW:2 * GW], ALU.add).then_inc(S("ry"), 1)
                v.wait_ge(S("gt"), B("gt", L) + 32)
                for c in range(2):
                    for i, t in enumerate(tiles):
                        v.wait_ge(S("op"), B("op", L) + c * len(tiles) + i + 1)
                        s = 0 if t < CT else 1
                        q = c * len(tiles) + i
                        v.tensor_tensor(hrow[:, q % 2, 0:CH], ps[:, t, :], tabs[:, s, c * CH:(c + 1) * CH], ALU.mult).then_inc(S("og"), 1)
                        v.wait_ge(S("og"), B("og", L) + q + 1)
                        v.tensor_tensor(xs[:, t, c * CH:(c + 1) * CH], xs[:, t, c * CH:(c + 1) * CH], hrow[:, q % 2, 0:CH], ALU.add).then_inc(S("xo"), 1)
                v.wait_ge(S("xo"), B("xo", L) + 2 * len(tiles))
                norm(1, tiles, lambda i, t: h2[:, t, :], False)
                for j in range(2 * PH):
                    v.wait_ge(S("fs"), B("fs", L) + j + 1)
                    b = 4 + 2 * (j % 2)
                    if j >= 2:
                        v.wait_ge(S(f"sd{j % 2}"), B(f"sd{j % 2}", L) + 16 * (j // 2))
                    v.tensor_copy(stage[:, j % 2, lo * P:TOK], ps[:, b:b + 2, :].rearrange("p a b -> p (a b)")[:, lo * P:TOK]).then_inc(S("fse"), 1)
                v.wait_ge(S("fse"), B("fse", L) + 2 * PH)

                def choose_keys(h, w):
                    s = scn[:, 2 * h + w, :]
                    link.then_max(v.max(v12[:, w, 0:8], s))
                    v.max_index(i12[:, w, 0:8], v12[:, w, 0:8], s)
                    link.then_max(v.match_replace(tk[:, w, :], v12[:, w, 0:8], s, -3e38))
                    link.then_max(v.max(v12[:, w, 8:16], tk[:, w, :]))
                    link.then_max(v.max_index(i12[:, w, 8:16], v12[:, w, 8:16], tk[:, w, :]))

                def choose_pairs(h):
                    v.tensor_copy(i12f, i12)
                    link.then_max(v.tensor_tensor(cand, v12[:, 0, :].unsqueeze(2).to_broadcast([P, TOPK, TOPK]),
                                         v12[:, 1, :].unsqueeze(1).to_broadcast([P, TOPK, TOPK]), ALU.add))
                    s = cand.rearrange("p a b -> p (a b)")
                    link.then_max(v.max(top[:, h, 0:8], s))
                    v.max_index(pos[:, 0:8], top[:, h, 0:8], s)
                    link.then_max(v.match_replace(cand2, top[:, h, 0:8], s, -3e38))
                    link.then_max(v.max(top[:, h, 8:16], cand2))
                    link(v.max_index(pos[:, 8:16], top[:, h, 8:16], cand2))
                    v.tensor_single_scalar(pab[:, 0, :], pos, 4, ALU.logical_shift_right)
                    link(v.tensor_single_scalar(pab[:, 1, :], pos, 15, ALU.bitwise_and))
                    link(v.tensor_copy(pabf, pab))
                    for w in range(2):
                        link(v.tensor_tensor(oh, pabf[:, w, :].unsqueeze(2).to_broadcast([P, TOPK, TOPK]),
                                             iota[:, :].unsqueeze(1).to_broadcast([P, TOPK, TOPK]), ALU.is_equal))
                        link(v.tensor_tensor(oh, oh, i12f[:, w, :].unsqueeze(1).to_broadcast([P, TOPK, TOPK]), ALU.mult))
                        link(v.reduce_sum(sel[:, w, :], oh, AX))
                    link(v.tensor_scalar(sel[:, 0, :], sel[:, 0, :], float(NKEYS), float(L * EXPERTS), ALU.mult, ALU.add))
                    return v.tensor_tensor(idxn[:, h, :], sel[:, 0, :], sel[:, 1, :], ALU.add)

                def gates_ahead(n_):
                    v.tensor_tensor(gx[:, 0, :].rearrange("p (h k) -> p h k", k=TOPK), top, top[:, :, 0:1].to_broadcast([P, PH, TOPK]), ALU.subtract).then_inc(S("gx"), 1)
                    v.wait_ge(S("ge"), B("ge", L) + n_ + 1)
                    g3 = gx[:, 1, :].rearrange("p (h k) -> p h k", k=TOPK)
                    link(v.reduce_sum(gs[:, 0, :], g3, AX))
                    link(v.reciprocal(gs[:, 1, :], gs[:, 0, :]))
                    link(v.tensor_tensor(gx[:, 0, :].rearrange("p (h k) -> p h k", k=TOPK), g3, gs[:, 1, :].unsqueeze(2).to_broadcast([P, PH, TOPK]), ALU.mult))

                def indices_out():
                    v.tensor_copy(istage[:, :], idxn.rearrange("p h k -> p (h k)")).then_inc(S("istg"), 1)

                v.wait_ge(S("sl"), B("sl", L) + 16)
                for h in range(PH):
                    choose_keys(h, 0)
                    choose_keys(h, 1)
                    last = choose_pairs(h)
                    link(last) if h < PH - 1 else last.then_inc(S("topk"), 1)
                v.wait_ge(S("topk"), B("topk", L) + 1)
                indices_out()
                gates_ahead(0)
                v.wait_ge(S("gt2"), B("gt2", L) + 32)
                NQ = SLOTS // BATCH

                def tile_body(i, s, ahead):
                    t = i + lo
                    v.tensor_copy(gstage[:, :], gx[:, 0, :])
                    v.tensor_copy(xt, h2[:, bass.ds(t, 1), :].rearrange("p a b -> p (a b)")).then_inc(S("stg"), 1)
                    v.wait_ge(S("stg"), B("stg", L) + i + 1)

                    def diagonals(q):
                        v.wait_ge(S("gel"), B("gel", L) + NQ * i + q + 1)
                        for s_ in range(q * BATCH, (q + 1) * BATCH):
                            if s_ >= 8:
                                v.wait_ge(S("em"), B("em", L) + SLOTS * i + s_ - 7)
                            v.tensor_scalar(dg[:, s_ % 8, :], ident[:, :], agel[:, s_:s_ + 1], gstage[:, s_:s_ + 1], ALU.mult, ALU.mult).then_inc(S("dg"), 1)

                    if ahead:
                        v.wait_ge(S("sl"), B("sl", L) + 16 * i + 32)
                    for q in range(NQ):
                        for s_ in range(q * BATCH, (q + 1) * BATCH):
                            uses = slot_uses(s_ % UVRING)
                            v.wait_ge(S(f"uv{s_ % UVRING}"), B(f"uv{s_ % UVRING}", L) + 16 * uses * i + 16 * (s_ // UVRING + 1))
                            m = v.tensor_tensor_reduce(uvr[:, s_ % UVRING, 0:D], xt, uvr[:, s_ % UVRING, 0:D], 1.0, 0.0, ALU.mult, ALU.add, adot[:, s_:s_ + 1])
                        m.then_inc(S("dot"), 1)
                        if q:
                            diagonals(q - 1)
                        h, part = q // CHOOSE_EVERY // 3, q // CHOOSE_EVERY % 3
                        if ahead and q % CHOOSE_EVERY == 0 and h < PH and part < 2:
                            choose_keys(h, part)
                        if ahead and q % CHOOSE_EVERY == 0 and h < PH and part == 2:
                            last = choose_pairs(h)
                            if h < PH - 1:
                                link.then_max(last)
                            else:
                                last.then_inc(S("topk"), 1)
                                v.wait_ge(S("topk"), B("topk", L) + i + 2)
                        if ahead and q == GATES_AT + 1:
                            gates_ahead(i + 1)
                    if ahead:
                        indices_out()
                    diagonals(NQ - 1)
                    v.wait_ge(S("em"), B("em", L) + SLOTS * i + SLOTS)
                    gj = gjunk.rearrange("p (a b) -> p a b", b=512)
                    v.tensor_tensor(gj, ps[:, 0:2, :], gtab[:, s, :].rearrange("p (a b) -> p a b", b=512), ALU.mult).then_inc(S("xa"), 1)
                    v.wait_ge(S("xa"), B("xa", L) + i + 1)
                    xrow = xs[:, bass.ds(t, 1), :].rearrange("p a b -> p (a b)")
                    v.tensor_tensor(xrow, xrow, gjunk, ALU.add).then_inc(S("xf"), 1)
                    v.wait_ge(S("xf"), B("xf", L) + i + 1)

                if lo == 0:
                    for i in link.loop(0, CT, CHOOSE_STEPS * PH + 2):
                        tile_body(i, 0, True)
                for i in link.loop(CT - lo, len(tiles) - 1, CHOOSE_STEPS * PH + 2):
                    tile_body(i, 1, True)
                tile_body(len(tiles) - 1, 1, False)
                v.sem_inc(S("layer"), 1)
            v.wait_ge(S("frt"), 1)
            v.wait_ge(S("fg"), 16)
            link(v.reciprocal(stat[:, 2, CT:TILES], stat[:, 1, CT:TILES]))
            for t in range(CT, TILES):
                v.scalar_tensor_tensor(xs[:, t, :], xs[:, t, :], stat[:, 2, t:t + 1], gtab[:, 0, :], ALU.mult, ALU.mult).then_inc(S("fin"), 1)

        @block.gpsimd
        def _(g):
            for L in range(LAYERS):
                n = f"_{L}"
                lo = first_out[L]
                if L:
                    g.wait_ge(S("layer"), L)
                sm = S("small")

                def bc(src, k=P):
                    return src.partition_broadcast(k).rearrange("a b c -> a (b c)")

                g.dma_start(wkr[:, :, :], a["w_in"][L].rearrange("(k p) n -> p k n", p=P)[:, :, C_KR:C_KR + 32]).then_inc(sm, 16)
                g.dma_start(wukv[:, :], a["mla_w_ukv"][L]).then_inc(sm, 16)
                g.dma_start(keysT[:, :, :], a["keys"][L].rearrange("w d n -> d w n")).then_inc(sm, 16)
                g.dma_start(gkv[:, :], bc(a["mla_kv_norm_g"][L:L + 1, :])).then_inc(sm, 16)
                g.dma_start(beta[:, :], a["mix_beta"][L]).then_inc(sm, 16)
                g.dma_start(smallw[:, 0:4], bc(a["swa_sink"][L:L + 1, :])).then_inc(sm, 16)
                g.dma_start(smallw[:, 4:12], bc(a["decay_rows"][L:L + 1, :])).then_inc(sm, 16)
                g.dma_start(smallw[:, 12:16], a["decay_cols"][L]).then_inc(sm, 16)
                g.wait_ge(S("kte"), B("kte", L) + 1)
                for h in range(1, HEADS):
                    m = g.tensor_copy(km[HD:MLA_QK, h, :], km[HD:MLA_QK, 0, :])
                m.then_inc(S("krc"), 1)
                g.wait_ge(S("krc"), B("krc", L) + 1)
                g.wait_ge(S("kn"), B("kn", L) + HEADS)
                g.wait_ge(S("vmm"), B("vmm", L) + TILES)
                g.dma_start(rpbt.rearrange("p h r c -> p (h r c)"), a["rpb"][L]).then_inc(S("nt"), 16)
                g.dma_start(nmask.rearrange("p a b -> p (a b)"), a["c_na"]).then_inc(S("nt"), 16)
                g.wait_ge(S("nt"), B("nt", L) + 32)
                for j in range(4 * HEADS):
                    t, h = j // HEADS, j % HEADS
                    off = 16 + col_starts()[t] - 16 * t
                    if j >= 2:
                        g.wait_ge(S("a_nm"), att_base("na", L) + j - 1 + (0 if lo else CT * HEADS))
                    g.tensor_tensor(nbias[:, j % 2, :].rearrange("p (s r c) -> p s r c", r=ROWS, c=8),
                                    rpbt[:, h, :, off:off + 32].rearrange("p r (s c) -> p s r c", c=8),
                                    nmask[:, t, :].rearrange("p (s r c) -> p s r c", r=ROWS, c=8), ALU.add).then_inc(S("nb"), 1)
                g.wait_ge(S("a_yt"), att_base("na", L) // HEADS + TILES - lo)
                g.dma_start(gn, bc(a["ret_gn"][L:L + 1, :])).then_inc(S("rtab"), 16)
                g.dma_start(rtab.rearrange("p a b -> p (a b)"), a["c_ret"]).then_inc(S("rtab"), 16)
                def gathers(i, first):
                    g.wait_ge(S("istg"), B("istg", L) + i + 1)
                    g.sem_inc(S("asked"), 1)
                    for s in range(SLOTS):
                        if s >= UVRING or not first:
                            used = s - UVRING if s >= UVRING else s + UVRING * (slot_uses(s) - 1) - SLOTS
                            g.wait_ge(S("em"), B("em", L) + SLOTS * i + used + 1)
                            g.sem_inc(S("asked"), 1)
                        g.indirect_dma_start(uvr[:, s % UVRING, :], None, a["uv"],
                                             bass.IndirectOffsetOnAxis(ap=istage[:, s:s + 1], axis=0)).then_inc(S(f"uv{s % UVRING}"), 16)

                gathers(0, True)
                with g.Fori(1, TILES - lo) as i:
                    gathers(i, False)
            g.wait_ge(S("layer"), LAYERS)
            g.dma_start(gtab[:, 0, :], bc(a["final_norm_g"])).then_inc(S("fg"), 16)


_KERNEL_OUT = "out_0_dram"


def laid_out(inputs):
    x = {k: np.asarray(v) for k, v in inputs.items()}
    L = LAYERS
    p = {}
    p["x"] = x["x"][0]
    p["ctx"] = x["ctx"][0]
    p["c"] = np.stack([x["c_ctx"], x["c"][0]]).reshape(2, KD, P).transpose(2, 1, 0)
    for name in ("ada_w", "ada_b", "norm_mix_g", "w_in", "mla_kv_norm_g", "mla_w_ukv", "swa_sink", "w_out", "norm_ffn_g", "peer_wq"):
        p[name] = x[name]
    q = np.arange(P)
    dr = np.arange(ROWS)[None, :] - (q // 8 % ROWS)[:, None] + ROWS - 1
    dc = np.clip(np.arange(NA_PITCH)[None, :] - 16 - (8 * (q // HD) + q % 8)[:, None] + 15, 0, 30)
    rpb = x["na_rpb"][:, :, dr[:, :, None], dc[:, None, :]]
    p["rpb"] = rpb.transpose(0, 2, 1, 3, 4).reshape(L, P, HEADS * ROWS * NA_PITCH)
    p["decay_rows"] = np.concatenate([x["ret_decay_f"], x["ret_decay_b"]], 1)
    both = np.stack([x["ret_decay_f"], x["ret_decay_b"]], 2).reshape(L, 2, 2, 2)
    p["decay_cols"] = np.repeat(both.transpose(0, 2, 1, 3), HD, axis=1).reshape(L, P, 4)
    p["ret_gn"] = np.concatenate([x["ret_gn_f"], x["ret_gn_b"]], 1)
    p["mix_beta"] = x["mix_beta"].reshape(L, KD, P).transpose(0, 2, 1)
    p["keys"] = np.stack([x["peer_k1"], x["peer_k2"]], 1).transpose(0, 1, 3, 2)
    p["uv"] = np.concatenate([x["peer_u"], x["peer_v"]], 2).reshape(L * EXPERTS, 2 * D)
    p["final_norm_g"] = x["final_norm_g"][None]
    p.update(constants())
    return {k: np.ascontiguousarray(v) for k, v in p.items()}


def program(nc, p):
    a = {k: nc.dram_tensor(f"in_{k}_dram", v.shape, mybir.dt.from_np(v.dtype), kind="ExternalInput").ap() for k, v in p.items()}
    out = nc.dram_tensor(_KERNEL_OUT, (NLAT, D), F32, kind="ExternalOutput").ap()
    build(nc, a, out)


def kernel(**inputs):
    import concourse.bacc as bacc
    from concourse.bass_utils import run_bass_kernel_spmd as run

    p = laid_out(inputs)
    nc = bacc.Bacc("TRN2", target_bir_lowering=False, num_devices=1)
    program(nc, p)
    r = run(nc, [{f"in_{k}_dram": v for k, v in p.items()}], core_ids=[0])
    return r.results[0][_KERNEL_OUT].reshape(1, NLAT, D)
```

```python
from contextlib import ExitStack

import numpy as np

import concourse.bass as bass
from concourse import mybir

F32 = mybir.dt.float32
U32 = mybir.dt.uint32
ALU = mybir.AluOpType
ACT = mybir.ActivationFunctionType
AX = mybir.AxisListType.X

P = 128
D = 1024
KD = D // P
LAYERS = 2
NCTX, NLAT = 256, 512
TILES = (NCTX + NLAT) // P
CT = NCTX // P
TOK = NCTX + NLAT
HEADS, HD = 4, 64
GW = HEADS * HD
MLA_QK = 96
GRID = 64
ROWS = NLAT // GRID
NA_PITCH = 48
IN_WIDTH = 3104
C_QCKV, C_KR, C_SWA, C_NAQK, C_NAV_RQ, C_RKV, C_GATE = 0, 512, 544, 1056, 1568, 2080, 2592
IN_CHUNKS = (C_QCKV, C_SWA, C_NAQK, C_NAV_RQ, C_RKV, C_GATE)
CH = 512
GROUP_K = 4
WRING = 3
ADA_CHUNKS = 6 * D // CH
MOD_FIRST = 4
MOD_BEFORE_FFN = ((7, 8), (9,), (), (), (), ())
MOD_EARLY = (2, 5, 7, 10)
MOD_BETWEEN = ((4, 5, 6), (7,), (8,), (9,), (10,), (11,))
PH, NKEYS, TOPK = 8, 128, 16
SLOTS = PH * TOPK
EXPERTS = NKEYS * NKEYS
EPS = 1e-6
NEG = -1e30
MLA_SCALE = float(MLA_QK) ** -0.5
CHOOSE_FROM = 6
CHOOSE_EVERY = 2
CHOOSE_STEPS = 23
GATES_AT = 54
UVRING = 11
BATCH = 2


def col_starts():
    first = np.clip(np.arange(4) * 16 - 8, 0, GRID - 16)
    return [int(v) for v in np.minimum(first, GRID - 32)]


def na_mask():
    out = np.zeros((4, P, ROWS, 32), np.float32)
    p = np.arange(P)
    for j, cb in enumerate(col_starts()):
        q = 16 * j + 8 * (p // HD) + p % 8
        cs = np.clip(q - 8, 0, GRID - 16)[:, None]
        k = cb + np.arange(32)[None, :]
        ok = (k >= cs) & (k < cs + 16)
        out[j] = np.where(ok, 0.0, NEG)[:, None, :]
    return out.reshape(4, P, ROWS, 4, 8).transpose(0, 1, 3, 2, 4).reshape(4, P, 256)


def constants():
    i = np.arange(P)
    diff = (i[None, :] - i[:, None]).astype(np.float32)
    ret = np.stack([np.maximum(diff, 0), np.maximum(-diff, 0), (diff >= 0), (diff <= 0)], 1).astype(np.float32)
    pos = np.zeros((P, 2, P), np.float32)
    pos[:, 0], pos[:, 1] = i + 1, P - i
    kpos = np.zeros((P, 8), np.float32)
    kpos[:, :4], kpos[:, 4:] = (P - 1 - i)[:, None], i[:, None]
    swa = np.stack([np.where(diff >= 0, 0, NEG)[:, :], np.where(diff <= 0, 0, NEG)], 1).astype(np.float32)
    tok = np.arange(NLAT)
    grid = np.stack([tok // GRID, tok % GRID], -1).astype(np.float32)

    def rope(dim):
        quarter = dim // 4
        inv = np.float32(10000.0) ** (-np.arange(quarter, dtype=np.float32) / np.float32(quarter))
        ang = (grid[:, :, None] * inv.astype(np.float32)).astype(np.float32)
        both = np.stack([np.cos(ang), np.sin(ang)], 1).astype(np.float32)
        return both.reshape(NLAT // P, P, 4 * quarter).transpose(1, 0, 2)

    return {
        "c_ident": np.eye(P, dtype=np.float32),
        "c_ret": ret.reshape(P, 4 * P),
        "c_pos": np.concatenate([pos.reshape(P, 2 * P), kpos], 1),
        "c_swa": swa.reshape(P, 2 * P),
        "c_na": na_mask().transpose(1, 0, 2).reshape(P, 4 * 256).copy(),
        "c_rope16": np.ascontiguousarray(rope(32).reshape(P, -1)),
        "c_rope32": np.ascontiguousarray(rope(64).reshape(P, -1)),
        "c_iota": np.tile(np.arange(TOPK, dtype=np.float32), (P, 1)),
    }


class Chain:

    def __init__(self, eng, sem):
        self.eng, self.sem, self.n, self.turns = eng, sem, 0, 0

    def __call__(self, ins):
        self.n += 1
        ins.then_inc(self.sem, 1)
        self.eng.wait_ge(self.sem, self.turns + self.n)

    def then_max(self, ins):
        self(ins)
        self.eng.sem_inc(self.own, 1)

    def loop(self, first, end, per):
        before = self.n
        with self.eng.Fori(first, end) as i:
            self.turns = (i - first) * per
            yield i
        assert self.n == before + per, self.n - before
        self.turns, self.n = 0, before + per * (end - first)


def attention_items(kind, layer):
    items = []
    for t in range(CT if layer == LAYERS - 1 else 0, TILES):
        for h in range(HEADS):
            if t < CT:
                spans = [(0, NCTX)]
            elif kind == "mla":
                spans = [(0, TOK)]
            elif kind == "swa":
                lo, hi = max(t - 1, CT), min(t + 2, TILES)
                spans = [(0, NCTX), (lo * P, (hi - lo) * P)]
            else:
                spans = [(0, NCTX), (NCTX + ROWS * col_starts()[t - CT], 256)]
            items.append((t, h, spans))
    return items


def first_layer_counts():
    c = {}
    for value, names in (
        (TILES, "c0 c0r c1 c1r c4 c4e c5 c5d c5e ckn ckr cks kd qe qt rke rkt sqe sqt u vme vmm "
                "ge gx gr gv oc inner osq pfb rg rm ro ry rye ryt topk stg xa xf"),
        (TILES + 1, "istg"),
        (2 * TILES, "op og xo"),
        (4, "c2 c2e c3 c3e"),
        (HEADS, "kn kne qd qdt"),
        (1, "cd cke ckq ckt dabs dex dln kr krc kre krr krt krz kte lg kd8 st"),
        (2 * HEADS, "dt dtm"),
        (2 * PH, "fq fqe fs fse"),
        (ADA_CHUNKS, "mps mrow"),
        (4 * HEADS, "nb"),
        (16 * 2, "nt rtab gt gt2"),
        (16 * 8, "small"),
        (TILES - CT, "rope rop2"),
        (CT + 7, "vne vnt"),
        (16 * ADA_CHUNKS // 2, "ms0 ms1 ab0 ab1"),
        (16 * PH, "sd0 sd1"),
        (16 * (TILES - 1), "sl"),
        (TILES * SLOTS, "dg em"),
        (TILES * SLOTS // BATCH, "dot gel"),
    ):
        for name in names.split():
            c[name] = value
    for r in range(UVRING):
        c[f"uv{r}"] = 16 * TILES * slot_uses(r)
    return c


def slot_uses(r):
    return (SLOTS - 1 - r) // UVRING + 1


def att_base(kind, layer):
    per = [HEADS * TILES, HEADS * (TILES - CT)]
    return 3 * per[0] * layer + ("mla", "swa", "na").index(kind) * per[layer]


def nb_(which, layer):
    return 2 * TILES * layer + TILES * which


def width(spans):
    return sum(w for _, w in spans)


def build(nc, a, out):
    ctx = ExitStack()
    with ctx:
        def sb(name, shape, dt=F32):
            return ctx.enter_context(nc.sbuf_tensor(name, shape, dt))

        sems = {}

        def S(name):
            if name not in sems:
                sems[name] = ctx.enter_context(nc.semaphore(name))
            return sems[name]

        xs = sb("xs", [P, TILES, D])
        hT = sb("hT", [P, KD, TOK])
        yT = sb("yT", [P, KD, TOK])
        wring = sb("wring", [P, WRING, GROUP_K, CH])
        ident = sb("ident", [P, P])
        wkr = sb("wkr", [P, KD, 32])
        wukv = sb("wukv", [P, 512])
        keysT = sb("keysT", [P, 2, NKEYS])
        gkv = sb("gkv", [P, P])
        beta = sb("beta", [P, KD])
        smallw = sb("smallw", [P, 16])
        rope16 = sb("rope16", [P, 4, 2, 2, 8])
        rope32 = sb("rope32", [P, 4, 2, 2, 16])
        swam = sb("swam", [P, 2, P])
        iota = sb("iota", [P, TOPK])
        cT = sb("cT", [P, KD, 2])
        cE = sb("cE", [P, KD, 2])
        eps = sb("eps", [P, 1])
        ones = sb("ones", [P, 2])
        stat = sb("stat", [P, 4, 8])
        att = sb("att", [P, 6, 32])
        X_WORDS = 101 * 256
        X = sb("X", [P, X_WORDS])
        ps = ctx.enter_context(nc.psum_tensor("ps", [P, 8, 512], F32))

        def view(at, shape, dt=None):
            n = int(np.prod(shape))
            assert at + n <= X_WORDS, (at, shape)
            v = X[:, at:at + n]
            if dt is not None:
                v = v.bitcast(dt)
            if len(shape) == 2:
                v = v.rearrange("p (a b) -> p a b", b=shape[1])
            elif len(shape) == 3:
                v = v.rearrange("p (a b c) -> p a b c", b=shape[1], c=shape[2])
            elif len(shape) == 4:
                v = v.rearrange("p (a b c d) -> p a b c d", b=shape[1], c=shape[2], d=shape[3])
            return v

        K = 256
        qm = view(0, [HEADS, TOK]); km = view(12 * K, [HEADS, TOK]); vm = view(24 * K, [TILES, GW])
        sq = view(30 * K, [2, TOK]); sk = view(36 * K, [1, TOK]); vs = view(39 * K, [TILES, P])
        nq = view(42 * K, [2, TOK]); nk = view(48 * K, [2, TOK]); vn = view(54 * K, [9, GW])
        nbias = view(63 * K, [2, 256]); rpbt = view(65 * K, [HEADS, ROWS, NA_PITCH]); nmask = view(71 * K, [4, 256])
        pr = view(75 * K, [2, TOK]); pT = view(81 * K, [2, TOK])
        prow = view(87 * K, [3, CH]); yr = view(93 * K, [2, GW])
        ckvT = view(63 * K, [TOK]); ckv = view(66 * K, [TILES, P])
        rq = view(0, [2, TOK]); rk = view(6 * K, [2, TOK]); rkr = view(12 * K, [TILES, GW])
        rv = view(18 * K, [TILES, GW]); gate = view(24 * K, [TILES, 2 * GW])
        qd = view(42 * K, [2, 2, TOK]); dt_ = view(54 * K, [2, HEADS, P]); rtab = view(58 * K, [4, P])
        st = view(60 * K, [TILES, 4, P]); qdt = view(72 * K, [2, 2, P])
        kd = view(75 * K, [TILES, 2, GW]); pfb = view(75 * K, [2, 2, HEADS * P])
        on = view(87 * K, [3, 2 * GW]); osq = view(93 * K, [2 * GW]); gn = view(40 * K, [2 * GW])
        gates = view(42 * K, [2, D]); hrow = view(62 * K, [2, D]); junk = view(70 * K, [D])
        mrow = view(87 * K, [2, CH]); adab = view(91 * K, [2, CH])
        ptab = sb("ptab", [P, 2 * P + 8])
        krrow = view(69 * K, [TILES, MLA_QK])
        rsm = sb("rsm", [P, 64])
        qTb = view(48 * K, [2, TOK]); stage = view(88 * K, [2, TOK])
        uvr = view(0, [UVRING, 2 * D])
        scn = view(88 * K, [2 * PH, NKEYS])
        tk = view(96 * K, [2, NKEYS]); cand = view(97 * K, [TOPK, TOPK]); cand2 = view(98 * K, [TOPK * TOPK])
        oh = view(99 * K, [TOPK, TOPK]); v12 = view(100 * K, [2, TOPK]); i12 = view(100 * K + 32, [2, TOPK], U32)
        i12f = view(100 * K + 64, [2, TOPK]); pos = view(100 * K + 96, [TOPK], U32); pab = view(100 * K + 112, [2, TOPK], U32)
        pabf = view(100 * K + 144, [2, TOPK]); sel = view(100 * K + 176, [2, TOPK]); gs = view(100 * K + 208, [2, PH])
        top_1 = view(94 * K, [PH, TOPK]); idxn_1 = view(94 * K + SLOTS, [PH, TOPK])
        hflat = hT[:, :, :].rearrange("p a b -> p (a b)")
        mod_early = (view(36 * K, [2, CH]), view(96 * K, [2, CH]))
        mod_late = tuple(hflat[:, i * D:(i + 1) * D].rearrange("p (a b) -> p a b", b=CH) for i in range(2))

        def mod_place(M, c):
            rows, bias = (mrow, adab) if M == 0 else mod_early if c < MOD_EARLY[-1] else mod_late
            return rows[:, c % 2, :], bias[:, c % 2, :]

        h2 = yT[:, :, :].rearrange("p a b -> p (a b)").rearrange("p (t d) -> p t d", d=D)
        norm_tables = ((h2[:, 0:4, :], h2[:, 4, :]), (view(0, [4, D]), view(16 * K, [D])))
        xt = hflat[:, 0:D]; gjunk = hflat[:, D:2 * D]; gtab = hflat[:, 2 * D:4 * D].rearrange("p (a b) -> p a b", b=D)
        dg = hflat[:, 4 * D:5 * D].rearrange("p (a b) -> p a b", b=P)
        small = hflat[:, 5 * D:6 * D]
        adot = small[:, 0:SLOTS]; agel = small[:, SLOTS:2 * SLOTS]
        gstage = small[:, 2 * SLOTS:3 * SLOTS]; istage = small[:, 3 * SLOTS:4 * SLOTS].bitcast(U32)
        top = small[:, 4 * SLOTS:5 * SLOTS].rearrange("p (h k) -> p h k", k=TOPK)
        gx = small[:, 5 * SLOTS:7 * SLOTS].rearrange("p (a b) -> p a b", b=SLOTS)
        idxn = small[:, 7 * SLOTS:8 * SLOTS].rearrange("p (h k) -> p h k", k=TOPK)

        def by_columns(g):
            return wring[:, g % WRING, :, :].rearrange("p a b -> p (a b)").rearrange("p (k n) -> p k n", n=CH // 2)

        counts = first_layer_counts()

        def B(name, layer):
            return counts[name] if layer else 0

        scores_d = nc.dram_tensor("scores", (TILES, P, 2 * PH, NKEYS), F32, kind="Internal").ap()
        mods = nc.dram_tensor("mods", (LAYERS, 2, 6 * D), F32, kind="Internal").ap()

        block = ctx.enter_context(nc.Block())
        LAST = LAYERS - 1
        first_out = [0, CT]

        @block.sync
        def _(sp):
            sp.dma_start(cT[:, :, :], a["c"]).then_inc(S("c_in"), 16)
            done, halves = [], [0]

            def send(L, w, col, name, count, split):
                for half in range(2):
                    g = len(done)
                    if g >= WRING:
                        sp.wait_ge(S(done[g - WRING][0]), done[g - WRING][1])
                    w3 = w.rearrange("(k p) n -> p k n", p=P)
                    if split:
                        sp.dma_start(wring[:, g % WRING, :, :], w3[:, half * GROUP_K:(half + 1) * GROUP_K, col:col + CH]).then_inc(S(f"w{g % WRING}"), 16)
                    else:
                        c0 = col + half * CH // 2
                        sp.dma_start(by_columns(g), w3[:, :, c0:c0 + CH // 2]).then_inc(S(f"w{g % WRING}"), 16)
                    if split and half == 0:
                        halves[0] += 1
                        done.append(("w_half", halves[0]))
                    elif split:
                        done.append((name, B(name, L) + count))
                    else:
                        done.append((name, B(name, L) + count - (0 if half else 2)))

            send(0, a["ada_w"][0], 0, "mps", 1, True)
            sp.dma_start(ident[:, :], a["c_ident"]).then_inc(S("in"), 16)
            sp.dma_start(xs[:, 0:CT, :], a["ctx"].rearrange("(t p) d -> p t d", p=P)).then_inc(S("in"), 16)
            sp.dma_start(xs[:, CT:TILES, :], a["x"].rearrange("(t p) d -> p t d", p=P)).then_inc(S("in"), 16)
            sp.dma_start(swam[:, :, :], a["c_swa"].rearrange("p (a b) -> p a b", b=P)).then_inc(S("in"), 16)
            sp.dma_start(ptab[:, :], a["c_pos"]).then_inc(S("in"), 16)
            sp.dma_start(rope16[:, :, :, :, :].rearrange("p a b c d -> p (a b c d)"), a["c_rope16"]).then_inc(S("in"), 16)
            sp.dma_start(rope32[:, :, :, :, :].rearrange("p a b c d -> p (a b c d)"), a["c_rope32"]).then_inc(S("in"), 16)
            sp.dma_start(iota[:, :], a["c_iota"]).then_inc(S("in"), 16)
            for c in range(1, ADA_CHUNKS):
                send(0, a["ada_w"][0], c * CH, "mps", c + 1, True)
            for L in range(LAYERS):
                made = TILES - first_out[L]
                stream = [(a["w_in"][L], col, name, count, split) for col, name, count, split in (
                    (C_QCKV, "c0", TILES, True), (C_SWA, "c1", TILES, True), (C_NAQK, "c2", 4, False),
                    (C_NAV_RQ, "c3", 4, False), (C_RKV, "c4", TILES, True), (C_GATE, "c5", made, True))]
                after = {}
                if L < LAST:
                    mod = [(L + 1, a["ada_w"][L + 1], c * CH, "mps", c + 1, True) for c in range(ADA_CHUNKS)]
                    after = {len(stream) - 1: mod[:MOD_EARLY[1]], len(stream): mod[MOD_EARLY[1]:MOD_EARLY[2]], len(stream) + 1: mod[MOD_EARLY[2]:MOD_EARLY[3]]}
                stream += [(a["w_out"][L], c * CH, "op", (c + 1) * made, True) for c in range(2)]
                stream += [(a["peer_wq"][L], c * CH, "fq", 4 * (c + 1), False) for c in range(4)]
                for i, chunk in enumerate(stream):
                    send(L, *chunk)
                    for m in after.get(i, ()):
                        send(*m)
                if L < LAST:
                    for m in mod[MOD_EARLY[3]:]:
                        send(*m)
                lo = first_out[L]
                for q in range(2):
                    sp.wait_ge(S(f"sd{q}"), B(f"sd{q}", L) + 16 * PH)
                with sp.Fori(0, TILES - lo - 1) as i:
                    sp.wait_ge(S("topk"), B("topk", L) + i + 1)
                    sp.dma_start(scn, scores_d[bass.ds(i + lo + 1, 1)].rearrange("t p j n -> p (t j) n")).then_inc(S("sl"), 16)
            for t in range(TILES - CT):
                sp.wait_ge(S("fin"), t + 1)
                sp.dma_start(out[t * P:(t + 1) * P, :], xs[:, CT + t, :]).then_inc(S("out"), 16)
            sp.wait_ge(S("out"), 16 * (TILES - CT))

        @block.tensor
        def _(pe):
            wg = [0]

            def take(n=2):
                g = wg[0]
                for i in range(n):
                    pe.wait_ge(S(f"w{(g + i) % WRING}"), 16 * ((g + i) // WRING + 1))
                wg[0] += n
                return g

            def wsl(g, k, c0, c1):
                return wring[:, (g + k // GROUP_K) % WRING, k % GROUP_K, c0:c1]

            def rows_chunk(L, tiles, ready, between=None, ctx_from=0, free=None):
                for half in range(2):
                    g = take(1)
                    for kk in range(GROUP_K):
                        k = half * GROUP_K + kk
                        for i, t in enumerate(tiles):
                            if k == 0 and free:
                                pe.wait_ge(free[0], free[1] + i + 1)
                            c0 = ctx_from if L == LAST and t < CT else 0
                            m = pe.matmul(ps[:, t, c0:CH], hT_or_y[0][:, k, t * P:(t + 1) * P],
                                          wring[:, g % WRING, kk, c0:CH], start=(k == 0), stop=(k == KD - 1))
                            if k == KD - 1 and t != tiles[-1]:
                                m.then_inc(ready, 1)
                    if half == 0:
                        m.then_inc(S("w_half"), 1)
                        if between:
                            between()
                m.then_inc(ready, 1)

            hT_or_y = [hT]
            for L in range(LAYERS):
                n = f"_{L}"
                lo = first_out[L]
                def modulation(M, chunks):
                    for c in chunks:
                        g = take(2)
                        if c >= 2:
                            pe.wait_ge(S("mrow"), B("mrow", M) + c - 1)
                        for k in range(KD):
                            m = pe.matmul(ps[0:2, 6 + c % 2, :], cT[:, k, :], wsl(g, k, 0, CH), start=(k == 0), stop=False)
                            if k == GROUP_K - 1:
                                m.then_inc(S("w_half"), 1)
                        pe.wait_ge(S(f"ab{c % 2}"), B(f"ab{c % 2}", M) + 16 * (c // 2 + 1))
                        pe.matmul(ps[0:2, 6 + c % 2, :], ones[0:1, :], mod_place(M, c)[1][0:1, :],
                                  start=False, stop=True).then_inc(S("mps"), 1)

                if L:
                    pe.wait_ge(S("layer"), L)
                else:
                    pe.wait_ge(S("silu"), 1)
                    modulation(0, range(MOD_FIRST))
                    pe.wait_ge(S("in"), 16 * 8)

                def norm_transposes(tag, tiles, rows, between=None):
                    for i, t in enumerate(tiles):
                        if between:
                            between(i)
                        pe.wait_ge(S("n_h"), nb_(tag, L) + i + 1)
                        if i >= 2:
                            pe.wait_ge(S("n_hT"), nb_(tag, L) + i - 1)
                        for k in range(KD):
                            m = pe.transpose(ps[:, 2 * (i % 2) + k // 4, (k % 4) * P:(k % 4 + 1) * P],
                                             rows(i, t)[:, k * P:(k + 1) * P], ident[:, :])
                        m.then_inc(S("n_ht"), 1)

                norm_transposes(0, range(TILES), lambda i, t: hrow[:, i % 2, :],
                                None if L else lambda i: modulation(0, MOD_BETWEEN[i]))
                pe.wait_ge(S("mrow"), B("mrow", L) + ADA_CHUNKS)
                pe.wait_ge(S("n_hT"), nb_(0, L) + TILES)
                pe.wait_ge(S("small"), B("small", L) + 16 * 8)

                for t in range(TILES):
                    for k in range(KD):
                        m = pe.matmul(ps[:, 7, t * 32:(t + 1) * 32], hT[:, k, t * P:(t + 1) * P], wkr[:, k, :],
                                      start=(k == 0), stop=(k == KD - 1))
                m.then_inc(S("kr"), 1)
                rows_chunk(L, range(TILES), S("c0"), ctx_from=384)
                pe.wait_ge(S("kre"), B("kre", L) + 1)
                for t in range(lo, TILES):
                    pe.wait_ge(S("c0r"), B("c0r", L) + t - lo + 1)
                    if t >= CT:
                        pe.wait_ge(S("rope"), B("rope", L) + t - CT + 1)
                    if t >= lo + 2:
                        pe.wait_ge(S("qe"), B("qe", L) + t - lo - 1)
                    for h in range(HEADS):
                        m = pe.transpose(ps[0:MLA_QK, 6 + t % 2, h * P:(h + 1) * P],
                                         prow[:, t % 3, h * MLA_QK:(h + 1) * MLA_QK], ident[:, :])
                    m.then_inc(S("qt"), 1)
                pe.wait_ge(S("qe"), B("qe", L) + TILES - lo)
                pe.wait_ge(S("krr"), B("krr", L) + 1)
                for t in range(TILES):
                    m = pe.transpose(ps[0:MLA_QK, 6 + t // 4, (t % 4) * P:(t % 4 + 1) * P], krrow[:, t, :], ident[:, :])
                m.then_inc(S("krt"), 1)
                pe.wait_ge(S("ckn"), B("ckn", L) + TILES)
                for t in range(TILES):
                    m = pe.transpose(ps[:, 4 + t // 4, (t % 4) * P:(t % 4 + 1) * P], ckv[:, t, :], ident[:, :])
                m.then_inc(S("ckt"), 1)
                pe.wait_ge(S("cke"), B("cke", L) + 1)
                for h in range(HEADS):
                    if h >= 2:
                        pe.wait_ge(S("kne"), B("kne", L) + h - 1)
                    b = 2 * (h % 2)
                    pe.matmul(ps[0:HD, b, :], wukv[:, h * P:h * P + HD], ckvT[:, 0:512], start=True, stop=True)
                    pe.matmul(ps[0:HD, b + 1, 0:256], wukv[:, h * P:h * P + HD], ckvT[:, 512:768],
                              start=True, stop=True).then_inc(S("kn"), 1)
                wv = wukv[:, :].rearrange("p (h e) -> p h e", e=P)[:, :, HD:P]
                for t in range(TILES):
                    if t >= 2:
                        pe.wait_ge(S("vme"), B("vme", L) + t - 1)
                    pe.matmul(ps[:, 4 + t % 2, 0:GW], ckvT[:, t * P:(t + 1) * P], wv,
                              start=True, stop=True).then_inc(S("vmm"), 1)
                pe.wait_ge(S("vme"), B("vme", L) + TILES)
                pe.wait_ge(S("kne"), B("kne", L) + HEADS)
                pe.wait_ge(S("kte"), B("kte", L) + 1)
                rows_chunk(L, range(TILES), S("c1"), ctx_from=GW)
                for t in range(TILES):
                    pe.wait_ge(S("c1r"), B("c1r", L) + t + 1)
                    if t >= CT:
                        pe.wait_ge(S("rop2"), B("rop2", L) + t - CT + 1)
                    if t >= 2:
                        pe.wait_ge(S("sqe"), B("sqe", L) + t - 1)
                    for b in range(2 if t >= lo else 0):
                        pe.transpose(ps[:, 6 + t % 2, b * P:(b + 1) * P],
                                     prow[:, t % 3, b * P:(b + 1) * P],
                                     ident[:, :])
                    pe.transpose(ps[:, 6 + t % 2, 2 * P:3 * P], prow[:, t % 3, GW:GW + P],
                                 ident[:, :]).then_inc(S("sqt"), 1)
                pe.wait_ge(S("sqe"), B("sqe", L) + TILES)

                def attention(kind):
                    ab = att_base(kind, L)
                    items = attention_items(kind, L)
                    N = len(items)
                    if kind == "mla":
                        pe.wait_ge(S("krc"), B("krc", L) + 1)

                    def ops(t, h):
                        if kind == "mla":
                            return qm[0:MLA_QK, h, :], km[0:MLA_QK, h, :]
                        r0 = HD * (h // 2) if kind == "swa" else HD * (h % 2)
                        b = h % 2 if kind == "swa" else h // 2
                        q, k = (sq, sk) if kind == "swa" else (nq, nk)
                        return q[r0:r0 + HD, b, :], k[r0:r0 + HD, 0 if kind == "swa" else b, :]

                    def scores(i):
                        t, h, spans = items[i]
                        if i >= 2:
                            pe.wait_ge(S("a_exp"), ab + i - 1)
                        q, k = ops(t, h)
                        q = q[:, t * P:(t + 1) * P]
                        at = 0
                        for first, w in spans:
                            done = 0
                            while done < w:
                                c = min(w - done, 512 - at % 512)
                                m = pe.matmul(ps[:, 2 * (i % 2) + at // 512, at % 512:at % 512 + c], q,
                                              k[:, first + done:first + done + c], start=True, stop=True)
                                done += c
                                at += c
                        m.then_inc(S("a_s"), 1)

                    def turn(i):
                        w = width(items[i][2])
                        pe.wait_ge(S("a_exp"), ab + i + 1)
                        if i >= 1:
                            pe.wait_ge(S("a_pt"), ab + i)
                        for b in range(w // P):
                            m = pe.transpose(ps[:, 4 + b // 4, (b % 4) * P:(b % 4 + 1) * P],
                                             pr[:, i % 2, b * P:(b + 1) * P], ident[:, :])
                        m.then_inc(S("a_t"), 1)

                    def values(i):
                        t, h, spans = items[i]
                        pe.wait_ge(S("a_pt"), ab + i + 1)
                        if i >= 2:
                            pe.wait_ge(S("a_y"), ab + i - 1)
                        if i % HEADS == 1 and i > HEADS:
                            pe.wait_ge(S("a_ye"), ab // HEADS + i // HEADS)
                        rows = []
                        for first, w in spans:
                            if kind == "na" and first:
                                strip = CT + (first - NCTX) // HD
                                rows += [vn[:, strip, h * HD:(h + 1) * HD], vn[:, strip + 2, h * HD:(h + 1) * HD]]
                                continue
                            for tt in range(first // P, (first + w) // P):
                                if kind == "mla":
                                    rows.append(vm[:, tt, h * HD:(h + 1) * HD])
                                elif kind == "swa":
                                    rows.append(vs[:, tt, (h // 2) * HD:(h // 2 + 1) * HD])
                                else:
                                    rows.append(vn[:, tt, h * HD:(h + 1) * HD])
                        for b, v in enumerate(rows):
                            m = pe.matmul(ps[:, 6 + i % 2, 0:HD], pT[:, i % 2, b * P:(b + 1) * P], v,
                                          start=(b == 0), stop=(b == len(rows) - 1))
                        m.then_inc(S("a_o"), 1)

                    def turn_y(j):
                        pe.wait_ge(S("a_y"), ab + HEADS * (j + 1))
                        for b in range(2):
                            m = pe.transpose(ps[:, 7, b * P:(b + 1) * P], yr[:, j % 2, b * P:(b + 1) * P], ident[:, :])
                        m.then_inc(S("a_yt"), 1)

                    for i in range(N + 3):
                        if i < N:
                            scores(i)
                        if 1 <= i <= N:
                            turn(i - 1)
                        if 2 <= i <= N + 1:
                            values(i - 2)
                        if i >= 6 and i % HEADS == 2:
                            turn_y(i // HEADS - 1)
                    pe.wait_ge(S("a_ye"), ab // HEADS + N // HEADS)

                attention("mla")
                attention("swa")
                for b in range(4):
                    if b % 2 == 0:
                        g = take(1)
                    for k in range(KD):
                        m = pe.matmul(ps[:, b, :], by_columns(g)[:, k, b % 2 * P:(b % 2 + 1) * P], hT[:, k, NCTX:TOK], start=(k == 0), stop=(k == KD - 1))
                    for k in range(KD if lo == 0 or b >= 2 else 0):
                        m = pe.matmul(ps[:, 4 + b, 0:NCTX], by_columns(g)[:, k, b % 2 * P:(b % 2 + 1) * P],
                                      hT[:, k, 0:NCTX], start=(k == 0), stop=(k == KD - 1))
                    m.then_inc(S("c2"), 1)
                pe.wait_ge(S("c2e"), B("c2e", L) + 4)
                for b in range(4):
                    if b % 2 == 0:
                        g = take(1)
                    for k in range(KD):
                        m = pe.matmul(ps[:, b, :], by_columns(g)[:, k, b % 2 * P:(b % 2 + 1) * P], hT[:, k, NCTX:TOK], start=(k == 0), stop=(k == KD - 1))
                    for k in range(KD if lo == 0 or b < 2 else 0):
                        m = pe.matmul(ps[:, 4 + b, 0:NCTX], by_columns(g)[:, k, b % 2 * P:(b % 2 + 1) * P],
                                      hT[:, k, 0:NCTX], start=(k == 0), stop=(k == KD - 1))
                    m.then_inc(S("c3"), 1)
                pe.wait_ge(S("c3e"), B("c3e", L) + 4)
                for v in range(9):
                    if v >= 2:
                        pe.wait_ge(S("vne"), B("vne", L) + v - 1)
                    first = v * P if v < CT else NCTX + HD * (v - CT)
                    for b in range(2):
                        m = pe.transpose(ps[:, 6 + v % 2, b * P:(b + 1) * P], pr[:, b, first:first + P], ident[:, :])
                    m.then_inc(S("vnt"), 1)
                pe.wait_ge(S("vne"), B("vne", L) + 9)
                attention("na")
                rows_chunk(L, range(TILES), S("c4"))

                def turn_keys():
                    pe.wait_ge(S("c4e"), B("c4e", L) + TILES)
                    for t in range(TILES):
                        if t >= 2:
                            pe.wait_ge(S("rke"), B("rke", L) + t - 1)
                        for b in range(2):
                            m = pe.transpose(ps[:, 6 + t % 2, b * P:(b + 1) * P], rkr[:, t, b * P:(b + 1) * P], ident[:, :])
                        m.then_inc(S("rkt"), 1)

                tiles = list(range(lo, TILES))
                n = len(tiles)
                rows_chunk(L, tiles, S("c5"), turn_keys, free=(S("c4e"), B("c4e", L) + lo))
                pe.wait_ge(S("rke"), B("rke", L) + TILES)
                if L < LAST:
                    modulation(L + 1, range(0, MOD_EARLY[0]))
                for t in range(TILES):
                    pe.wait_ge(S("kd"), B("kd", L) + t + 1)
                    if t >= lo:
                        pe.wait_ge(S("c5e"), B("c5e", L) + t - lo + 1)
                    for b in range(2):
                        for d in range(2):
                            m = pe.matmul(ps[:, t, (2 * b + d) * P:(2 * b + d + 1) * P], kd[:, t, d, b * P:(b + 1) * P],
                                          rv[:, t, b * P:(b + 1) * P], start=True, stop=True)
                    m.then_inc(S("u"), 1)
                if L < LAST:
                    modulation(L + 1, range(MOD_EARLY[0], MOD_EARLY[1]))
                    pe.wait_ge(S("mrow"), B("mrow", L + 1) + MOD_EARLY[1])
                pe.wait_ge(S("st"), B("st", L) + 1)
                pe.wait_ge(S("qd"), B("qd", L) + 4)

                def turn_out(j):
                    pe.wait_ge(S("ry"), B("ry", L) + j + 1)
                    if j >= 2:
                        pe.wait_ge(S("rye"), B("rye", L) + j - 1)
                    for b in range(2):
                        m = pe.transpose(ps[:, 6 + j % 2, b * P:(b + 1) * P], on[:, j % 3, b * P:(b + 1) * P], ident[:, :])
                    m.then_inc(S("ryt"), 1)

                for i in range(n + 1):
                    if i < n:
                        t = tiles[i]
                        if i >= 2:
                            pe.wait_ge(S("pfb"), B("pfb", L) + i - 1)
                        for h in range(HEADS):
                            r0 = HD * (h % 2)
                            m = pe.matmul(ps[:, 2 * (i % 2) + h % 2, (h // 2) * P:(h // 2 + 1) * P], rk[r0:r0 + HD, h // 2, t * P:(t + 1) * P],
                                          rq[r0:r0 + HD, h // 2, t * P:(t + 1) * P], start=True, stop=True)
                        m.then_inc(S("inner"), 1)
                    if i >= 1:
                        t, j = tiles[i - 1], i - 1
                        pe.wait_ge(S("pfb"), B("pfb", L) + j + 1)
                        if j >= 2:
                            pe.wait_ge(S("oc"), B("oc", L) + j - 1)
                        for d in range(2):
                            for b in range(2):
                                o = ps[:, 4 + j % 2, d * GW + b * P:d * GW + (b + 1) * P]
                                pe.matmul(o, qd[:, b, d, t * P:(t + 1) * P], st[:, t, 2 * b + d, :], start=True, stop=False,
                                          skip_group_check=True)
                                for h in (2 * b, 2 * b + 1):
                                    m = pe.matmul(ps[:, 4 + j % 2, d * GW + h * HD:d * GW + (h + 1) * HD],
                                                  pfb[:, j % 2, d, h * P:(h + 1) * P], rv[:, t, h * HD:(h + 1) * HD],
                                                  start=False, stop=True, skip_group_check=True)
                        m.then_inc(S("ro"), 1)
                    if i >= 4:
                        turn_out(i - 4)
                pe.wait_ge(S("oc"), B("oc", L) + n)

                def last_outputs():
                    for j in range(n - 3, n):
                        turn_out(j)
                    pe.wait_ge(S("rye"), B("rye", L) + n)

                hT_or_y[0] = yT
                rows_chunk(L, tiles, S("op"), last_outputs)
                if L < LAST:
                    modulation(L + 1, range(MOD_EARLY[1], MOD_EARLY[2]))
                rows_chunk(L, tiles, S("op"), free=(S("og"), B("og", L)))
                hT_or_y[0] = hT
                pe.wait_ge(S("og"), B("og", L) + 2 * len(tiles))
                norm_transposes(1, tiles, lambda i, t: h2[:, t, :],
                                None if L == LAST else lambda i: modulation(L + 1, MOD_BEFORE_FFN[i]))
                pe.wait_ge(S("n_hT"), nb_(1, L) + len(tiles))
                for j in range(2 * PH):
                    if j % 2 == 0:
                        g = take(1)
                    if j >= 2:
                        pe.wait_ge(S("fqe"), B("fqe", L) + j - 1)
                    c0 = (j % 2) * P
                    for k in range(KD):
                        m = pe.matmul(ps[:, 2 * (j % 2), :], by_columns(g)[:, k, c0:c0 + P], hT[:, k, NCTX:TOK], start=(k == 0), stop=(k == KD - 1))
                    if lo == 0:
                        for k in range(KD):
                            m = pe.matmul(ps[:, 2 * (j % 2) + 1, 0:256], by_columns(g)[:, k, c0:c0 + P], hT[:, k, 0:NCTX],
                                          start=(k == 0), stop=(k == KD - 1))
                    m.then_inc(S("fq"), 1)
                    if j >= 1:
                        key_scores = j - 1
                        pe.wait_ge(S("fqe"), B("fqe", L) + key_scores + 1)
                        if key_scores >= 2:
                            pe.wait_ge(S("fse"), B("fse", L) + key_scores - 1)
                        for t in tiles:
                            m = pe.matmul(ps[:, 4 + 2 * (key_scores % 2) + t // 4, (t % 4) * P:(t % 4 + 1) * P],
                                          qTb[:, key_scores % 2, t * P:(t + 1) * P], keysT[:, key_scores % 2, :], start=True, stop=True)
                        m.then_inc(S("fs"), 1)
                j = 2 * PH - 1
                pe.wait_ge(S("fqe"), B("fqe", L) + j + 1)
                pe.wait_ge(S("fse"), B("fse", L) + j - 1)
                for t in tiles:
                    m = pe.matmul(ps[:, 4 + 2 * (j % 2) + t // 4, (t % 4) * P:(t % 4 + 1) * P],
                                  qTb[:, j % 2, t * P:(t + 1) * P], keysT[:, j % 2, :], start=True, stop=True)
                m.then_inc(S("fs"), 1)
                if L < LAST:
                    pe.wait_ge(S("fse"), B("fse", L) + 2 * PH)
                    modulation(L + 1, range(MOD_EARLY[3], ADA_CHUNKS))
                pe.wait_ge(S("fse"), B("fse", L) + 2 * PH)
                with pe.Fori(0, len(tiles)) as i:
                    pe.wait_ge(S("stg"), B("stg", L) + i + 1)
                    for s in range(SLOTS):
                        pe.wait_ge(S("dg"), B("dg", L) + SLOTS * i + s + 1)
                        for h in range(2):
                            m = pe.matmul(ps[:, h, :], dg[:, s % 8, :], uvr[:, s % UVRING, D + 512 * h:D + 512 * h + 512],
                                          start=(s == 0), stop=(s == SLOTS - 1))
                        m.then_inc(S("em"), 1)

        @block.scalar
        def _(act):
            link = Chain(act, S("act"))
            act.wait_ge(S("c_in"), 16)
            nc.scalar.activation(cE[:, :, :], cT[:, :, :], ACT.Exp, scale=-1.0).then_inc(S("ce"), 1)

            def last_squares(t):
                i = t - CT
                act.wait_ge(S("xf"), B("xf", LAST) + (i + 1 if t == TILES - 1 else TILES - 1 - CT))
                nc.scalar.activation(gjunk, xs[:, t, :], ACT.Square, accum_out=stat[:, 0, t:t + 1]).then_inc(S("fsq"), 1)
                act.wait_ge(S("fsq"), i + 1)
                nc.scalar.activation(stat[:, 1, t:t + 1], stat[:, 0, t:t + 1], ACT.Sqrt, scale=1.0 / D, bias=eps[:, 0:1]).then_inc(S("frt"), 1)

            for L in range(LAYERS):
                n = f"_{L}"
                lo = first_out[L]
                tiles = list(range(lo, TILES))
                if L:
                    act.wait_ge(S("layer"), L)

                def load_bias(M, c):
                    act.dma_start(mod_place(M, c)[1][0:1, :], a["ada_b"][M:M + 1, c * CH:(c + 1) * CH]).then_inc(S(f"ab{c % 2}"), 16)

                def modulation(M, chunks, end):
                    for c in chunks:
                        act.wait_ge(S("mps"), B("mps", M) + c + 1)
                        if c + 2 < end:
                            load_bias(M, c + 2)
                        if c >= 2:
                            act.wait_ge(S(f"ms{c % 2}"), B(f"ms{c % 2}", M) + 16 * (c // 2))
                        nc.scalar.activation(mod_place(M, c)[0][0:2, :], ps[0:2, 6 + c % 2, :], ACT.Copy).then_inc(S("mrow"), 1)
                        act.wait_ge(S("mrow"), B("mrow", M) + c + 1)
                        act.dma_start(mods[M, :, c * CH:(c + 1) * CH], mod_place(M, c)[0][0:2, :]).then_inc(S(f"ms{c % 2}"), 16)

                def squares(tag, tiles):
                    act.wait_ge(S("eps"), 1)
                    for i, t in enumerate(tiles):
                        if tag:
                            act.wait_ge(S("xo"), B("xo", L) + len(tiles) + i + 1)
                        nc.scalar.activation(junk, xs[:, t, :], ACT.Square, accum_out=stat[:, 0, t:t + 1]).then_inc(S("n_sq"), 1)
                        act.wait_ge(S("n_sq"), nb_(tag, L) + i + 1)
                        nc.scalar.activation(stat[:, 1, t:t + 1], stat[:, 0, t:t + 1], ACT.Sqrt, scale=1.0 / D, bias=eps[:, 0:1]).then_inc(S("n_rt"), 1)

                def load_tables(M, tag, chunks):
                    for q in range(2):
                        act.wait_ge(S(f"ms{q}"), B(f"ms{q}", M) + 16 * (chunks // 2))
                    tabs, gain = norm_tables[tag]
                    for s in range(2):
                        for w, c in ((0, 3 * tag + 1), (1, 3 * tag)):
                            act.dma_start(tabs[:, 2 * s + w, :], mods[M, s:s + 1, c * D:(c + 1) * D].partition_broadcast(P).rearrange("a b c -> a (b c)")).then_inc(S("n_tab"), 16)
                    g = a["norm_ffn_g"] if tag else a["norm_mix_g"]
                    act.dma_start(gain, g[M:M + 1, :].partition_broadcast(P).rearrange("a b c -> a (b c)")).then_inc(S("n_tab"), 16)

                if L == 0:
                    load_bias(0, 0)
                    load_bias(0, 1)
                    modulation(0, range(2), ADA_CHUNKS)
                    act.wait_ge(S("in"), 16 * 8)
                    squares(0, range(TILES))
                    modulation(0, range(2, MOD_FIRST), ADA_CHUNKS)

                def norm(tag, tiles, between=None):
                    for i, t in enumerate(tiles):
                        if between:
                            between(i)
                        act.wait_ge(S("n_ht"), nb_(tag, L) + i + 1)
                        b = 2 * (i % 2)
                        nc.scalar.activation(hT[:, :, t * P:(t + 1) * P],
                                             ps[:, b:b + 2, :].rearrange("p a (k q) -> p (a k) q", q=P), ACT.Copy).then_inc(S("n_hT"), 1)

                if L:
                    squares(0, range(TILES))
                    norm(0, range(TILES))
                else:
                    load_tables(0, 0, MOD_FIRST)
                    norm(0, range(TILES), lambda i: modulation(0, MOD_BETWEEN[i], ADA_CHUNKS))
                for q in range(2):
                    act.wait_ge(S(f"ms{q}"), B(f"ms{q}", L) + 16 * (ADA_CHUNKS // 2))
                act.wait_ge(S("kr"), B("kr", L) + 1)
                act.wait_ge(S("krz"), B("krz", L) + 1)
                nc.scalar.activation(krrow[:, :, HD:MLA_QK], ps[:, 7, 0:6 * 32].rearrange("p (t q) -> p t q", q=32), ACT.Copy).then_inc(S("kre"), 1)

                def q_out(t):
                    act.wait_ge(S("qt"), B("qt", L) + t - lo + 1)
                    nc.scalar.activation(qm[0:MLA_QK, :, t * P:(t + 1) * P],
                                         ps[0:MLA_QK, 6 + t % 2, :].rearrange("p (h q) -> p h q", q=P), ACT.Copy).then_inc(S("qe"), 1)

                for t in range(TILES):
                    act.wait_ge(S("c0"), B("c0", L) + t + 1)
                    nc.scalar.activation(ckv[:, t, :], ps[:, t, 384:512], ACT.Copy).then_inc(S("ckr"), 1)
                    if t >= lo + 3:
                        act.wait_ge(S("qt"), B("qt", L) + t - lo - 2)
                    if t >= lo:
                        nc.scalar.activation(prow[:, t % 3, 0:384], ps[:, t, 0:384], ACT.Copy).then_inc(S("c0r"), 1)
                    if t > lo:
                        q_out(t - 1)
                q_out(TILES - 1)
                act.wait_ge(S("krt"), B("krt", L) + 1)
                nc.scalar.activation(km[HD:MLA_QK, 0, :], ps[HD:MLA_QK, 6:8, :].rearrange("p a b -> p (a b)")[:, 0:TOK], ACT.Copy).then_inc(S("kte"), 1)
                act.wait_ge(S("cks"), B("cks", L) + TILES)
                nc.scalar.activation(stat[:, 1, 0:TILES], stat[:, 0, 0:TILES], ACT.Sqrt, scale=1.0 / P, bias=eps[:, 0:1]).then_inc(S("ckq"), 1)
                act.wait_ge(S("ckt"), B("ckt", L) + 1)
                nc.scalar.activation(ckvT, ps[:, 4:6, :].rearrange("p a b -> p (a b)")[:, 0:TOK], ACT.Copy).then_inc(S("cke"), 1)
                for h in range(HEADS):
                    act.wait_ge(S("kn"), B("kn", L) + h + 1)
                    b = 2 * (h % 2)
                    nc.scalar.activation(km[0:HD, h, :], ps[0:HD, b:b + 2, :].rearrange("p a b -> p (a b)")[:, 0:TOK], ACT.Copy).then_inc(S("kne"), 1)

                def sq_out(t):
                    act.wait_ge(S("sqt"), B("sqt", L) + t + 1)
                    if t >= lo:
                        nc.scalar.activation(sq[:, :, t * P:(t + 1) * P], ps[:, 6 + t % 2, 0:2 * P].rearrange("p (b q) -> p b q", q=P), ACT.Copy, scale=0.125)
                    nc.scalar.activation(sk[:, 0, t * P:(t + 1) * P], ps[:, 6 + t % 2, 2 * P:3 * P], ACT.Copy).then_inc(S("sqe"), 1)

                for t in range(TILES):
                    act.wait_ge(S("c1"), B("c1", L) + t + 1)
                    if t >= 3:
                        act.wait_ge(S("sqt"), B("sqt", L) + t - 2)
                    else:
                        act.wait_ge(S("qt"), B("qt", L) + TILES - lo)
                    nc.scalar.activation(vs[:, t, :], ps[:, t, 384:512], ACT.Copy)
                    if t >= lo:
                        nc.scalar.activation(prow[:, t % 3, 0:GW].rearrange("p (r g d) -> p g r d", g=2, r=2),
                                             ps[:, t, 0:GW].rearrange("p (g r d) -> p g r d", g=2, r=2), ACT.Copy)
                    nc.scalar.activation(prow[:, t % 3, GW:384], ps[:, t, GW:384], ACT.Copy).then_inc(S("c1r"), 1)
                    if t:
                        sq_out(t - 1)
                sq_out(TILES - 1)

                def attention(kind):
                    ab = att_base(kind, L)
                    items = attention_items(kind, L)
                    N = len(items)

                    def y_out(j):
                        act.wait_ge(S("a_yt"), ab // HEADS + j + 1)
                        t = items[HEADS * j][0]
                        kb = {"mla": 0, "swa": 2, "na": 4}[kind]
                        for b in range(2):
                            src = ps[:, 7, b * P:(b + 1) * P]
                            if kind == "na" and t >= CT:
                                s0 = 2 * (t - CT)
                                dst = yT[:, kb + b, NCTX:TOK].rearrange("p (r s c) -> p s r c", r=ROWS, c=8)[:, s0:s0 + 2]
                                src = src.rearrange("p (s r c) -> p s r c", s=2, c=8)
                            else:
                                dst = yT[:, kb + b, t * P:(t + 1) * P]
                            m = nc.scalar.activation(dst, src, ACT.Copy, scale=beta[:, kb + b:kb + b + 1])
                        m.then_inc(S("a_ye"), 1)

                    for i in range(N + 3):
                        if i < N:
                            w = width(items[i][2])
                            act.wait_ge(S("a_nm"), ab + i + 1)
                            if i >= 2:
                                act.wait_ge(S("a_t"), ab + i - 1)
                            c = i % 32
                            if kind == "swa":
                                nc.scalar.activation(att[:, 3, c:c + 1], smallw[:, items[i][1]:items[i][1] + 1], ACT.Exp, bias=att[:, 1, c:c + 1])
                            nc.scalar.activation(pr[:, i % 2, 0:w], ps[:, 2 * (i % 2):2 * (i % 2) + 2, :].rearrange("p a b -> p (a b)")[:, 0:w],
                                                 ACT.Exp, scale=MLA_SCALE if kind == "mla" else 1.0,
                                                 bias=att[:, 1, c:c + 1], accum_out=att[:, 2, c:c + 1]).then_inc(S("a_exp"), 1)
                        if i >= 6 and i % HEADS == 2:
                            y_out(i // HEADS - 1)

                attention("mla")
                attention("swa")
                def by_strip(x):
                    return x.rearrange("p (s r c) -> p r s c", r=ROWS, c=8)

                for b in range(4):
                    act.wait_ge(S("c2"), B("c2", L) + b + 1)
                    dst, s = (nq, 0.125) if b < 2 else (nk, 1.0)
                    m = nc.scalar.activation(by_strip(dst[:, b % 2, NCTX:TOK]), ps[:, b, :].rearrange("p (r s c) -> p r s c", r=ROWS, c=8), ACT.Copy, scale=s)
                    if lo == 0 or b >= 2:
                        m = nc.scalar.activation(dst[:, b % 2, 0:NCTX], ps[:, 4 + b, 0:NCTX], ACT.Copy, scale=s)
                    m.then_inc(S("c2e"), 1)
                for b in range(4):
                    act.wait_ge(S("c3"), B("c3", L) + b + 1)
                    if b < 2:
                        nc.scalar.activation(by_strip(pr[:, b, NCTX:TOK]), ps[:, b, :].rearrange("p (r s c) -> p r s c", r=ROWS, c=8), ACT.Copy)
                        nc.scalar.activation(pr[:, b, 0:NCTX], ps[:, 4 + b, 0:NCTX], ACT.Copy).then_inc(S("c3e"), 1)
                    else:
                        m = nc.scalar.activation(rq[:, b - 2, NCTX:TOK], ps[:, b, :], ACT.Copy)
                        if lo == 0:
                            m = nc.scalar.activation(rq[:, b - 2, 0:NCTX], ps[:, 4 + b, 0:NCTX], ACT.Copy)
                        m.then_inc(S("c3e"), 1)
                for v in range(9):
                    act.wait_ge(S("vnt"), B("vnt", L) + v + 1)
                    nc.scalar.activation(vn[:, v, :], ps[:, 6 + v % 2, 0:GW], ACT.Copy).then_inc(S("vne"), 1)
                attention("na")
                for t in range(TILES):
                    act.wait_ge(S("c4"), B("c4", L) + t + 1)
                    nc.scalar.activation(rkr[:, t, :], ps[:, t, 0:GW], ACT.Copy, scale=0.125)
                    nc.scalar.activation(rv[:, t, :], ps[:, t, GW:2 * GW], ACT.Copy).then_inc(S("c4e"), 1)
                dec = smallw[:, 4:16]
                act.wait_ge(S("dabs"), B("dabs", L) + 1)
                nc.scalar.activation(rsm[:, 12:24], rsm[:, 0:12], ACT.Exp, scale=-1.0).then_inc(S("dex"), 1)
                act.wait_ge(S("dex"), B("dex", L) + 1)
                nc.scalar.activation(rsm[:, 24:36], rsm[:, 12:24], ACT.Ln, bias=1.0).then_inc(S("dln"), 1)
                act.wait_ge(S("lg"), B("lg", L) + 1)
                nc.scalar.activation(rsm[:, 56:64], rsm[:, 48:56], ACT.Exp).then_inc(S("kd8"), 1)
                nc.scalar.activation(rsm[:, 0:4], rsm[:, 44:48], ACT.Exp, scale=float(P)).then_inc(S("cd"), 1)
                act.wait_ge(S("rtab"), B("rtab", L) + 32)
                for d in range(2):
                    for h in range(HEADS):
                        c = 36 + 4 * d + h
                        nc.scalar.activation(dt_[:, d, h, :], rtab[:, d, :], ACT.Exp, scale=rsm[:, c:c + 1]).then_inc(S("dt"), 1)
                for b in range(2):
                    for d in range(2):
                        c = 44 + 2 * b + d
                        nc.scalar.activation(qdt[:, b, d, :], ptab[:, d * P:(d + 1) * P], ACT.Exp, scale=rsm[:, c:c + 1]).then_inc(S("qdt"), 1)
                for t in range(TILES):
                    act.wait_ge(S("rkt"), B("rkt", L) + t + 1)
                    nc.scalar.activation(rk[:, :, t * P:(t + 1) * P], ps[:, 6 + t % 2, 0:2 * P].rearrange("p (b q) -> p b q", q=P), ACT.Copy).then_inc(S("rke"), 1)
                if L < LAST:
                    load_bias(L + 1, 0)
                    load_bias(L + 1, 1)
                for i, t in enumerate(tiles):
                    act.wait_ge(S("c5"), B("c5", L) + i + 1)
                    nc.scalar.activation(gate[:, t, :], ps[:, t, :], ACT.Silu).then_inc(S("c5e"), 1)
                if L < LAST:
                    modulation(L + 1, range(0, MOD_EARLY[1]), MOD_EARLY[3])
                for j in range(len(tiles) + 4):
                    if j < len(tiles):
                        act.wait_ge(S("oc"), B("oc", L) + j + 1)
                        if j:
                            act.wait_ge(S("gv"), B("gv", L) + j)
                        nc.scalar.activation(osq, on[:, j % 3, :], ACT.Square).then_inc(S("osq"), 1)
                    if 1 <= j <= len(tiles):
                        act.wait_ge(S("gv"), B("gv", L) + j)
                        nc.scalar.activation(rsm[:, 20:28], rsm[:, 12:20], ACT.Sqrt, scale=1.0 / HD, bias=eps[:, 0:1]).then_inc(S("gr"), 1)
                    if j >= 4:
                        q, t = j - 4, tiles[j - 4]
                        act.wait_ge(S("ryt"), B("ryt", L) + q + 1)
                        for b in range(2):
                            m = nc.scalar.activation(yT[:, 6 + b, t * P:(t + 1) * P], ps[:, 6 + q % 2, b * P:(b + 1) * P], ACT.Copy, scale=beta[:, 6 + b:7 + b])
                        m.then_inc(S("rye"), 1)
                for s in range(2):
                    act.dma_start(gates[:, s, :], mods[L, s:s + 1, 2 * D:3 * D].partition_broadcast(P).rearrange("a b c -> a (b c)")).then_inc(S("gt"), 16)
                load_tables(L, 1, ADA_CHUNKS)
                if L < LAST:
                    modulation(L + 1, range(MOD_EARLY[1], MOD_EARLY[2]), MOD_EARLY[3])
                squares(1, tiles)
                norm(1, tiles, None if L == LAST else lambda i: modulation(L + 1, MOD_BEFORE_FFN[i], MOD_EARLY[3]))
                def store_scores(j):
                    act.wait_ge(S("fse"), B("fse", L) + j + 1)
                    act.dma_start(scores_d[lo:TILES, :, j, :].rearrange("t p n -> p t n"),
                                  stage[:, j % 2, lo * P:TOK].rearrange("p (t n) -> p t n", n=NKEYS)).then_inc(S(f"sd{j % 2}"), 16)

                for j in range(2 * PH):
                    if j >= 2:
                        store_scores(j - 2)
                    act.wait_ge(S("fq"), B("fq", L) + j + 1)
                    if j >= 2:
                        act.wait_ge(S("fs"), B("fs", L) + j - 1)
                    if lo == 0:
                        nc.scalar.activation(qTb[:, j % 2, 0:NCTX], ps[:, 2 * (j % 2) + 1, 0:256], ACT.Copy)
                    nc.scalar.activation(qTb[:, j % 2, NCTX:TOK], ps[:, 2 * (j % 2), :], ACT.Copy).then_inc(S("fqe"), 1)
                store_scores(2 * PH - 2)
                store_scores(2 * PH - 1)
                for s in range(2):
                    row = a["final_norm_g"] if L == LAST and s == 0 else mods[L, s:s + 1, 5 * D:6 * D]
                    act.dma_start(gtab[:, s, :], row.partition_broadcast(P).rearrange("a b c -> a (b c)")).then_inc(S("gt2"), 16)
                if L < LAST:
                    load_bias(L + 1, MOD_EARLY[3])
                    load_bias(L + 1, MOD_EARLY[3] + 1)
                    modulation(L + 1, range(MOD_EARLY[3], ADA_CHUNKS), ADA_CHUNKS)
                act.wait_ge(S("gx"), B("gx", L) + 1)
                nc.scalar.activation(gx[:, 1, :], gx[:, 0, :], ACT.Exp).then_inc(S("ge"), 1)

                def expert_gelus(i, ahead):
                    for q in range(SLOTS // BATCH):
                        act.wait_ge(S("dot"), B("dot", L) + (SLOTS // BATCH) * i + q + 1)
                        nc.scalar.activation(agel[:, q * BATCH:(q + 1) * BATCH], adot[:, q * BATCH:(q + 1) * BATCH], ACT.Gelu).then_inc(S("gel"), 1)
                        if ahead and q == GATES_AT:
                            act.wait_ge(S("gx"), B("gx", L) + i + 2)
                            nc.scalar.activation(gx[:, 1, :], gx[:, 0, :], ACT.Exp).then_inc(S("ge"), 1)

                with act.Fori(0, len(tiles) - 1) as i:
                    expert_gelus(i, True)
                if L < LAST:
                    act.wait_ge(S("stg"), B("stg", L) + len(tiles))
                    load_tables(L + 1, 0, ADA_CHUNKS)
                if L == LAST:
                    for t in range(CT, TILES - 1):
                        last_squares(t)
                expert_gelus(len(tiles) - 1, False)
            last_squares(TILES - 1)

        @block.vector
        def _(v):
            link = Chain(v, S("dve"))
            link.own = S("max_steps")
            v.memset(ones[:, :], 1.0)
            v.memset(eps[:, :], EPS).then_inc(S("eps"), 1)
            v.wait_ge(S("ce"), 1)
            link(v.tensor_scalar(cE[:, :, :], cE[:, :, :], 1.0, None, ALU.add))
            link(v.reciprocal(cE[:, :, :], cE[:, :, :]))
            v.tensor_tensor(cT[:, :, :], cT[:, :, :], cE[:, :, :], ALU.mult).then_inc(S("silu"), 1)

            def last_norm(t):
                v.wait_ge(S("frt"), t - CT + 1)
                link(v.reciprocal(stat[:, 2, t:t + 1], stat[:, 1, t:t + 1]))
                v.scalar_tensor_tensor(xs[:, t, :], xs[:, t, :], stat[:, 2, t:t + 1], gtab[:, 0, :], ALU.mult, ALU.mult).then_inc(S("fin"), 1)

            for L in range(LAYERS):
                n = f"_{L}"
                lo = first_out[L]
                tiles = list(range(lo, TILES))

                def scale_tables(M, tag):
                    v.wait_ge(S("n_tab"), 16 * 5 * (2 * M + tag + 1))
                    tabs, gain = norm_tables[tag]
                    for s in range(2):
                        m = v.scalar_tensor_tensor(tabs[:, 2 * s, :], tabs[:, 2 * s, :], 1.0, gain, ALU.add, ALU.mult)
                    m.then_inc(S("n_scale"), 1)

                def norm(tag, tiles, rows, free):
                    v.wait_ge(S("n_scale"), 2 * L + tag + 1)
                    tabs, gain = norm_tables[tag]
                    for i, t in enumerate(tiles):
                        s = 0 if t < CT else 1
                        r = rows(i, t)
                        v.wait_ge(S("n_rt"), nb_(tag, L) + i + 1)
                        link(v.reciprocal(stat[:, 2, t:t + 1], stat[:, 1, t:t + 1]))
                        if free and i >= 2:
                            v.wait_ge(S("n_ht"), nb_(tag, L) + i - 1)
                        link(v.scalar_tensor_tensor(r, xs[:, t, :], stat[:, 2, t:t + 1], tabs[:, 2 * s, :], ALU.mult, ALU.mult))
                        v.tensor_tensor(r, r, tabs[:, 2 * s + 1, :], ALU.add).then_inc(S("n_h"), 1)

                if L == 0:
                    v.wait_ge(S("in"), 16 * 8)
                    scale_tables(0, 0)
                norm(0, range(TILES), lambda i, t: hrow[:, i % 2, :], True)

                def rope(x1, x2, cos, sin, tmp):
                    v.tensor_tensor(tmp[0], x1, cos, ALU.mult)
                    v.tensor_tensor(tmp[1], x2, sin, ALU.mult)
                    v.tensor_tensor(tmp[2], x1, sin, ALU.mult)
                    link(v.tensor_tensor(tmp[3], x2, cos, ALU.mult))
                    v.tensor_tensor(x1, tmp[0], tmp[1], ALU.subtract)
                    return v.tensor_tensor(x2, tmp[2], tmp[3], ALU.add)

                v.wait_ge(S("n_hT"), nb_(0, L) + TILES)
                v.memset(krrow, 0.0).then_inc(S("krz"), 1)
                v.wait_ge(S("kre"), B("kre", L) + 1)
                kk = krrow[:, CT:TILES, HD:MLA_QK].rearrange("p t (x r q) -> p t x r q", x=2, r=2)
                tmp = pr[:, 0, 0:256].rearrange("p (i t x q) -> p i t x q", i=4, t=4, x=2)
                rope(kk[:, :, :, 0, :], kk[:, :, :, 1, :], rope16[:, :, 0, :, :], rope16[:, :, 1, :, :],
                     [tmp[:, i] for i in range(4)]).then_inc(S("krr"), 1)
                for t in range(TILES):
                    v.wait_ge(S("ckr"), B("ckr", L) + t + 1)
                    v.tensor_tensor_reduce(pT[:, 0, 0:P], ckv[:, t, :], ckv[:, t, :], 1.0, 0.0, ALU.mult, ALU.add, stat[:, 0, t:t + 1]).then_inc(S("cks"), 1)
                    v.wait_ge(S("cks"), B("cks", L) + t + 1)
                    if t >= CT:
                        v.wait_ge(S("c0r"), B("c0r", L) + t - lo + 1)
                        xq = prow[:, t % 3, 0:384].rearrange("p (h q) -> p h q", q=MLA_QK)[:, :, HD:MLA_QK].rearrange("p h (x r q) -> p h x r q", x=2, r=2)
                        bc = [rope16[:, t - CT, w, :, :].unsqueeze(1).to_broadcast([P, HEADS, 2, 8]) for w in range(2)]
                        tmp = pr[:, 0, 0:256].rearrange("p (i t x q) -> p i t x q", i=4, t=4, x=2)
                        rope(xq[:, :, :, 0, :], xq[:, :, :, 1, :], bc[0], bc[1], [tmp[:, i] for i in range(4)]).then_inc(S("rope"), 1)
                        v.wait_ge(S("rope"), B("rope", L) + t - CT + 1)
                v.wait_ge(S("ckq"), B("ckq", L) + 1)
                v.wait_ge(S("small"), B("small", L) + 16 * 8)
                link(v.reciprocal(stat[:, 2, 0:TILES], stat[:, 1, 0:TILES]))
                for t in range(TILES):
                    v.scalar_tensor_tensor(ckv[:, t, :], ckv[:, t, :], stat[:, 2, t:t + 1], gkv[:, :], ALU.mult, ALU.mult).then_inc(S("ckn"), 1)
                for t in range(TILES):
                    v.wait_ge(S("vmm"), B("vmm", L) + t + 1)
                    v.tensor_copy(vm[:, t, :], ps[:, 4 + t % 2, 0:GW]).then_inc(S("vme"), 1)
                for t in range(CT, TILES):
                    v.wait_ge(S("c1r"), B("c1r", L) + t + 1)
                    xq = prow[:, t % 3, 0:384].rearrange("p (h x r q) -> p h x r q", h=6, x=2, r=2)
                    bc = [rope32[:, t - CT, w, :, :].unsqueeze(1).to_broadcast([P, 6, 2, 16]) for w in range(2)]
                    tmp = pr[:, 0, 0:768].rearrange("p (i t x q) -> p i t x q", i=4, t=6, x=2)
                    rope(xq[:, :, :, 0, :], xq[:, :, :, 1, :], bc[0], bc[1], [tmp[:, i] for i in range(4)]).then_inc(S("rop2"), 1)
                    v.wait_ge(S("rop2"), B("rop2", L) + t - CT + 1)

                def attention(kind):
                    ab = att_base(kind, L)
                    items = attention_items(kind, L)
                    N = len(items)
                    for i in range(N + 2):
                        if i < N:
                            t, h, spans = items[i]
                            w = width(spans)
                            c = i % 32
                            flat = ps[:, 2 * (i % 2):2 * (i % 2) + 2, :].rearrange("p a b -> p (a b)")
                            v.wait_ge(S("a_s"), ab + i + 1)
                            if kind == "swa" and t >= CT:
                                if t > CT:
                                    link(v.tensor_tensor(flat[:, 256:384], flat[:, 256:384], swam[:, 0, :], ALU.add))
                                if t < TILES - 1:
                                    link(v.tensor_tensor(flat[:, w - P:w], flat[:, w - P:w], swam[:, 1, :], ALU.add))
                            if kind == "na" and t >= CT:
                                j = i - (0 if lo else CT * HEADS)
                                v.wait_ge(S("nb"), B("nb", L) + j + 1)
                                link(v.tensor_tensor(flat[:, 256:512], flat[:, 256:512], nbias[:, j % 2, :], ALU.add))
                            link(v.reduce_max(att[:, 0, c:c + 1], flat[:, 0:w], AX))
                            if kind == "swa":
                                v.tensor_scalar(att[:, 1, c:c + 1], att[:, 0, c:c + 1], smallw[:, h:h + 1], -1.0, ALU.max, ALU.mult).then_inc(S("a_nm"), 1)
                            else:
                                v.tensor_scalar(att[:, 1, c:c + 1], att[:, 0, c:c + 1], -MLA_SCALE if kind == "mla" else -1.0, None, ALU.mult).then_inc(S("a_nm"), 1)
                        if 1 <= i <= N:
                            j = i - 1
                            w = width(items[j][2])
                            v.wait_ge(S("a_t"), ab + j + 1)
                            if j >= 2:
                                v.wait_ge(S("a_o"), ab + j - 1)
                            v.tensor_copy(pT[:, j % 2, 0:w], ps[:, 4:6, :].rearrange("p a b -> p (a b)")[:, 0:w]).then_inc(S("a_pt"), 1)
                        if i >= 2:
                            j = i - 2
                            c = j % 32
                            g = j // HEADS
                            h = items[j][1]
                            total = att[:, 2, c:c + 1]
                            if kind == "swa":
                                link(v.tensor_tensor(att[:, 4, c:c + 1], att[:, 2, c:c + 1], att[:, 3, c:c + 1], ALU.add))
                                total = att[:, 4, c:c + 1]
                            link(v.reciprocal(att[:, 5, c:c + 1], total))
                            v.wait_ge(S("a_o"), ab + j + 1)
                            if h == 0 and g >= 2:
                                v.wait_ge(S("a_yt"), ab // HEADS + g - 1)
                            v.tensor_scalar(yr[:, g % 2, h * HD:(h + 1) * HD], ps[:, 6 + j % 2, 0:HD],
                                            att[:, 5, c:c + 1], None, ALU.mult).then_inc(S("a_y"), 1)

                attention("mla")
                attention("swa")
                attention("na")
                link(v.tensor_scalar(rsm[:, 12:24], smallw[:, 4:16], -1.0, None, ALU.mult))
                v.tensor_tensor(rsm[:, 0:12], rsm[:, 12:24], smallw[:, 4:16], ALU.max).then_inc(S("dabs"), 1)
                v.wait_ge(S("dln"), B("dln", L) + 1)
                link(v.tensor_scalar(rsm[:, 0:12], smallw[:, 4:16], 0.0, None, ALU.min))
                link(v.tensor_tensor(rsm[:, 36:48], rsm[:, 0:12], rsm[:, 24:36], ALU.subtract))
                v.tensor_tensor(rsm[:, 48:56], rsm[:, 36:44], ptab[:, 2 * P:2 * P + 8], ALU.mult).then_inc(S("lg"), 1)
                for i in range(8):
                    d, h = i // 4, i % 4
                    v.wait_ge(S("dt"), B("dt", L) + i + 1)
                    v.tensor_tensor(dt_[:, d, h, :], dt_[:, d, h, :], rtab[:, 2 + d, :], ALU.mult).then_inc(S("dtm"), 1)
                for i in range(4):
                    b, d = i // 2, i % 2
                    v.wait_ge(S("qdt"), B("qdt", L) + i + 1)
                    v.tensor_tensor(qd[:, b, d, lo * P:TOK].rearrange("p (t q) -> p t q", q=P), rq[:, b, lo * P:TOK].rearrange("p (t q) -> p t q", q=P),
                                    qdt[:, b, d, :].unsqueeze(1).to_broadcast([P, TILES - lo, P]), ALU.mult).then_inc(S("qd"), 1)
                v.wait_ge(S("kd8"), B("kd8", L) + 1)
                v.wait_ge(S("rtab"), B("rtab", L) + 32)
                for t in range(TILES):
                    v.wait_ge(S("c4e"), B("c4e", L) + t + 1)
                    for d in range(2):
                        m = v.tensor_tensor(kd[:, t, d, :].rearrange("p (h e) -> p h e", e=HD), rkr[:, t, :].rearrange("p (h e) -> p h e", e=HD),
                                            rsm[:, 56 + 4 * d:60 + 4 * d].unsqueeze(2).to_broadcast([P, HEADS, HD]), ALU.mult)
                    m.then_inc(S("kd"), 1)
                link(v.memset(st, 0.0))
                v.wait_ge(S("cd"), B("cd", L) + 1)
                for step in range(TILES - 1):
                    for d, order in ((0, [0, 1, 2, 3, 4, 5]), (1, [1, 0, 5, 4, 3, 2])):
                        was, now = order[step], order[step + 1]
                        v.wait_ge(S("u"), B("u", L) + (TILES if d else was + 1))
                        for b in range(2):
                            c = 2 * b + d
                            for r0 in (0, HD):
                                last = v.scalar_tensor_tensor(st[r0:r0 + HD, now, c, r0:r0 + HD], st[r0:r0 + HD, was, c, r0:r0 + HD], rsm[r0:r0 + HD, c:c + 1],
                                                              ps[r0:r0 + HD, was, c * P + r0:c * P + r0 + HD], ALU.mult, ALU.add)
                    link(last) if step < TILES - 2 else last.then_inc(S("st"), 1)
                v.wait_ge(S("dtm"), B("dtm", L) + 8)
                n = len(tiles)
                for j in range(n + 3):
                    if j < n:
                        v.wait_ge(S("inner"), B("inner", L) + j + 1)
                        if j >= 2:
                            v.wait_ge(S("ro"), B("ro", L) + j - 1)
                        for d in range(2):
                            m = v.tensor_tensor(pfb[:, j % 2, d, :].rearrange("p (b w q) -> p b w q", b=2, w=2),
                                                ps[:, 2 * (j % 2):2 * (j % 2) + 2, 0:2 * P].rearrange("p w (b q) -> p b w q", b=2),
                                                dt_[:, d, :, :].rearrange("p (b w) q -> p b w q", w=2), ALU.mult)
                        m.then_inc(S("pfb"), 1)
                    if 1 <= j <= n:
                        q = j - 1
                        v.wait_ge(S("ro"), B("ro", L) + q + 1)
                        if q >= 3:
                            v.wait_ge(S("ryt"), B("ryt", L) + q - 2)
                        if q:
                            v.wait_ge(S("oc"), B("oc", L) + q)
                        po = ps[:, 4 + q % 2, :].rearrange("p (g e) -> p g e", e=HD)
                        link(v.reduce_sum(rsm[:, 4:12], po, AX))
                        link(v.tensor_scalar(rsm[:, 4:12], rsm[:, 4:12], 1.0 / HD, None, ALU.mult))
                        v.tensor_tensor(on[:, q % 3, :].rearrange("p (g e) -> p g e", e=HD), po,
                                        rsm[:, 4:12].unsqueeze(2).to_broadcast([P, 8, HD]), ALU.subtract).then_inc(S("oc"), 1)
                    if j >= 3:
                        q = j - 3
                        v.wait_ge(S("gr"), B("gr", L) + q + 1)
                        if q:
                            v.wait_ge(S("rm"), B("rm", L) + q)
                        link(v.reciprocal(rsm[:, 28:36], rsm[:, 20:28]))
                        o = on[:, q % 3, :].rearrange("p (g e) -> p g e", e=HD)
                        v.tensor_tensor(o, o, rsm[:, 28:36].unsqueeze(2).to_broadcast([P, 8, HD]), ALU.mult).then_inc(S("rm"), 1)
                    if 2 <= j <= n + 1:
                        q = j - 2
                        v.wait_ge(S("osq"), B("osq", L) + q + 1)
                        v.reduce_sum(rsm[:, 12:20], osq.rearrange("p (g e) -> p g e", e=HD), AX).then_inc(S("gv"), 1)
                scale_tables(L, 1)
                v.wait_ge(S("gt"), B("gt", L) + 32)
                for c in range(2):
                    for i, t in enumerate(tiles):
                        v.wait_ge(S("op"), B("op", L) + c * len(tiles) + i + 1)
                        s = 0 if t < CT else 1
                        q = c * len(tiles) + i
                        v.tensor_tensor(hrow[:, q % 2, 0:CH], ps[:, t, :], gates[:, s, c * CH:(c + 1) * CH], ALU.mult).then_inc(S("og"), 1)
                        v.wait_ge(S("og"), B("og", L) + q + 1)
                        v.tensor_tensor(xs[:, t, c * CH:(c + 1) * CH], xs[:, t, c * CH:(c + 1) * CH], hrow[:, q % 2, 0:CH], ALU.add).then_inc(S("xo"), 1)
                v.wait_ge(S("xo"), B("xo", L) + 2 * len(tiles))
                norm(1, tiles, lambda i, t: h2[:, t, :], False)
                def choose_keys(scores, halves):
                    for w in halves:
                        m = v.max(v12[:, w, 0:8], scores(w))
                    link.then_max(m)
                    for w in halves:
                        v.max_index(i12[:, w, 0:8], v12[:, w, 0:8], scores(w))
                        m = v.match_replace(tk[:, w, :], v12[:, w, 0:8], scores(w), -3e38)
                    link.then_max(m)
                    for w in halves:
                        m = v.max(v12[:, w, 8:16], tk[:, w, :])
                    link.then_max(m)
                    for w in halves:
                        m = v.max_index(i12[:, w, 8:16], v12[:, w, 8:16], tk[:, w, :])
                    link.then_max(m)

                def choose_pairs(top, idxn, h):
                    v.tensor_copy(i12f, i12)
                    link.then_max(v.tensor_tensor(cand, v12[:, 0, :].unsqueeze(2).to_broadcast([P, TOPK, TOPK]),
                                         v12[:, 1, :].unsqueeze(1).to_broadcast([P, TOPK, TOPK]), ALU.add))
                    s = cand.rearrange("p a b -> p (a b)")
                    link.then_max(v.max(top[:, h, 0:8], s))
                    v.max_index(pos[:, 0:8], top[:, h, 0:8], s)
                    link.then_max(v.match_replace(cand2, top[:, h, 0:8], s, -3e38))
                    link.then_max(v.max(top[:, h, 8:16], cand2))
                    link(v.max_index(pos[:, 8:16], top[:, h, 8:16], cand2))
                    v.tensor_single_scalar(pab[:, 0, :], pos, 4, ALU.logical_shift_right)
                    link(v.tensor_single_scalar(pab[:, 1, :], pos, 15, ALU.bitwise_and))
                    link(v.tensor_copy(pabf, pab))
                    for w in range(2):
                        link(v.tensor_tensor(oh, pabf[:, w, :].unsqueeze(2).to_broadcast([P, TOPK, TOPK]),
                                             iota[:, :].unsqueeze(1).to_broadcast([P, TOPK, TOPK]), ALU.is_equal))
                        link(v.tensor_tensor(oh, oh, i12f[:, w, :].unsqueeze(1).to_broadcast([P, TOPK, TOPK]), ALU.mult))
                        link(v.reduce_sum(sel[:, w, :], oh, AX))
                    link(v.tensor_scalar(sel[:, 0, :], sel[:, 0, :], float(NKEYS), float(L * EXPERTS), ALU.mult, ALU.add))
                    return v.tensor_tensor(idxn[:, h, :], sel[:, 0, :], sel[:, 1, :], ALU.add)

                def gates_ahead(n_):
                    v.tensor_tensor(gx[:, 0, :].rearrange("p (h k) -> p h k", k=TOPK), top, top[:, :, 0:1].to_broadcast([P, PH, TOPK]), ALU.subtract).then_inc(S("gx"), 1)
                    v.wait_ge(S("ge"), B("ge", L) + n_ + 1)
                    g3 = gx[:, 1, :].rearrange("p (h k) -> p h k", k=TOPK)
                    link(v.reduce_sum(gs[:, 0, :], g3, AX))
                    link(v.reciprocal(gs[:, 1, :], gs[:, 0, :]))
                    link(v.tensor_tensor(gx[:, 0, :].rearrange("p (h k) -> p h k", k=TOPK), g3, gs[:, 1, :].unsqueeze(2).to_broadcast([P, PH, TOPK]), ALU.mult))

                def indices_out(idxn, first=0, end=SLOTS):
                    v.tensor_copy(istage[:, first:end], idxn.rearrange("p h k -> p (h k)")[:, first:end]).then_inc(S("istg"), 1)

                early = (PH - 1) * TOPK
                for j in range(2 * PH):
                    v.wait_ge(S("fs"), B("fs", L) + j + 1)
                    if j == 2 * PH - 1:
                        if L < LAST:
                            for q in range(2):
                                v.wait_ge(S(f"ms{q}"), B(f"ms{q}", L + 1) + 16 * (MOD_EARLY[3] // 2))
                        indices_out(idxn_1, 0, early)
                    b = 4 + 2 * (j % 2)
                    if j >= 2:
                        v.wait_ge(S(f"sd{j % 2}"), B(f"sd{j % 2}", L) + 16 * (j // 2))
                    v.tensor_copy(stage[:, j % 2, lo * P:TOK], ps[:, b:b + 2, :].rearrange("p a b -> p (a b)")[:, lo * P:TOK]).then_inc(S("fse"), 1)
                    if j % 2:
                        v.wait_ge(S("fse"), B("fse", L) + j + 1)
                        choose_keys(lambda w: stage[:, w, lo * P:(lo + 1) * P], (0, 1))
                        last = choose_pairs(top_1, idxn_1, j // 2)
                        link(last)

                link(v.tensor_copy(top, top_1))
                indices_out(idxn_1, early)
                v.wait_ge(S("istg"), B("istg", L) + 2)
                v.sem_inc(S("topk"), 1)
                gates_ahead(0)
                if L < LAST:
                    for q in range(2):
                        v.wait_ge(S(f"ms{q}"), B(f"ms{q}", L + 1) + 16 * (ADA_CHUNKS // 2))
                NQ = SLOTS // BATCH

                def tile_body(i, s, ahead, last_one=False):
                    t = i + lo
                    v.tensor_copy(gstage[:, :], gx[:, 0, :])
                    v.tensor_copy(xt, h2[:, bass.ds(t, 1), :].rearrange("p a b -> p (a b)")).then_inc(S("stg"), 1)
                    v.wait_ge(S("stg"), B("stg", L) + i + 1)

                    def diagonals(q):
                        v.wait_ge(S("gel"), B("gel", L) + NQ * i + q + 1)
                        for s_ in range(q * BATCH, (q + 1) * BATCH):
                            if s_ >= 8:
                                v.wait_ge(S("em"), B("em", L) + SLOTS * i + s_ - 7)
                            v.tensor_scalar(dg[:, s_ % 8, :], ident[:, :], agel[:, s_:s_ + 1], gstage[:, s_:s_ + 1], ALU.mult, ALU.mult).then_inc(S("dg"), 1)

                    for q in range(NQ):
                        if ahead and q == CHOOSE_FROM:
                            v.wait_ge(S("sl"), B("sl", L) + 16 * i + 16)
                        for s_ in range(q * BATCH, (q + 1) * BATCH):
                            uses = slot_uses(s_ % UVRING)
                            v.wait_ge(S(f"uv{s_ % UVRING}"), B(f"uv{s_ % UVRING}", L) + 16 * uses * i + 16 * (s_ // UVRING + 1))
                            m = v.tensor_tensor_reduce(uvr[:, s_ % UVRING, 0:D], xt, uvr[:, s_ % UVRING, 0:D], 1.0, 0.0, ALU.mult, ALU.add, adot[:, s_:s_ + 1])
                        m.then_inc(S("dot"), 1)
                        if q:
                            diagonals(q - 1)
                        step = (q - CHOOSE_FROM) // CHOOSE_EVERY
                        h, part = step // 3, step % 3
                        if ahead and (q - CHOOSE_FROM) % CHOOSE_EVERY == 0 and 0 <= h < PH and part < 2:
                            choose_keys(lambda w: scn[:, 2 * h + w, :], (part,))
                        if ahead and (q - CHOOSE_FROM) % CHOOSE_EVERY == 0 and 0 <= h < PH and part == 2:
                            last = choose_pairs(top, idxn, h)
                            if h < PH - 1:
                                link.then_max(last)
                            else:
                                last.then_inc(S("topk"), 1)
                                v.wait_ge(S("topk"), B("topk", L) + i + 2)
                        if last_one and L < LAST and q == NQ // 2:
                            scale_tables(L + 1, 0)
                        if last_one and L == LAST and q == NQ // 2:
                            v.wait_ge(S("gt2"), B("gt2", L) + 32)
                            for t_ in range(CT, TILES - 1):
                                last_norm(t_)
                        if ahead and q == GATES_AT + 1:
                            gates_ahead(i + 1)
                    if ahead:
                        indices_out(idxn)
                    diagonals(NQ - 1)
                    v.wait_ge(S("em"), B("em", L) + SLOTS * i + SLOTS)
                    v.wait_ge(S("gt2"), B("gt2", L) + 32)
                    gj = gjunk.rearrange("p (a b) -> p a b", b=512)
                    v.tensor_tensor(gj, ps[:, 0:2, :], gtab[:, s, :].rearrange("p (a b) -> p a b", b=512), ALU.mult).then_inc(S("xa"), 1)
                    v.wait_ge(S("xa"), B("xa", L) + i + 1)
                    xrow = xs[:, bass.ds(t, 1), :].rearrange("p a b -> p (a b)")
                    v.tensor_tensor(xrow, xrow, gjunk, ALU.add).then_inc(S("xf"), 1)
                    v.wait_ge(S("xf"), B("xf", L) + i + 1)

                if lo == 0:
                    for i in link.loop(0, CT, CHOOSE_STEPS * PH + 2):
                        tile_body(i, 0, True)
                for i in link.loop(CT - lo, len(tiles) - 1, CHOOSE_STEPS * PH + 2):
                    tile_body(i, 1, True)
                tile_body(len(tiles) - 1, 1, False, last_one=True)
                v.sem_inc(S("layer"), 1)
            last_norm(TILES - 1)

        @block.gpsimd
        def _(g):
            for L in range(LAYERS):
                n = f"_{L}"
                lo = first_out[L]
                if L:
                    g.wait_ge(S("layer"), L)
                sm = S("small")

                def bc(src, k=P):
                    return src.partition_broadcast(k).rearrange("a b c -> a (b c)")

                g.dma_start(wkr[:, :, :], a["w_in"][L].rearrange("(k p) n -> p k n", p=P)[:, :, C_KR:C_KR + 32]).then_inc(sm, 16)
                g.dma_start(wukv[:, :], a["mla_w_ukv"][L]).then_inc(sm, 16)
                g.dma_start(keysT[:, :, :], a["keys"][L].rearrange("w d n -> d w n")).then_inc(sm, 16)
                g.dma_start(gkv[:, :], bc(a["mla_kv_norm_g"][L:L + 1, :])).then_inc(sm, 16)
                g.dma_start(beta[:, :], a["mix_beta"][L]).then_inc(sm, 16)
                g.dma_start(smallw[:, 0:4], bc(a["swa_sink"][L:L + 1, :])).then_inc(sm, 16)
                g.dma_start(smallw[:, 4:12], bc(a["decay_rows"][L:L + 1, :])).then_inc(sm, 16)
                g.dma_start(smallw[:, 12:16], a["decay_cols"][L]).then_inc(sm, 16)
                g.wait_ge(S("kte"), B("kte", L) + 1)
                for h in range(1, HEADS):
                    m = g.tensor_copy(km[HD:MLA_QK, h, :], km[HD:MLA_QK, 0, :])
                m.then_inc(S("krc"), 1)
                g.wait_ge(S("krc"), B("krc", L) + 1)
                g.wait_ge(S("kn"), B("kn", L) + HEADS)
                g.wait_ge(S("vmm"), B("vmm", L) + TILES)
                g.dma_start(rpbt.rearrange("p h r c -> p (h r c)"), a["rpb"][L]).then_inc(S("nt"), 16)
                g.dma_start(nmask.rearrange("p a b -> p (a b)"), a["c_na"]).then_inc(S("nt"), 16)
                g.wait_ge(S("nt"), B("nt", L) + 32)
                for j in range(4 * HEADS):
                    t, h = j // HEADS, j % HEADS
                    off = 16 + col_starts()[t] - 16 * t
                    if j >= 2:
                        g.wait_ge(S("a_nm"), att_base("na", L) + j - 1 + (0 if lo else CT * HEADS))
                    g.tensor_tensor(nbias[:, j % 2, :].rearrange("p (s r c) -> p s r c", r=ROWS, c=8),
                                    rpbt[:, h, :, off:off + 32].rearrange("p r (s c) -> p s r c", c=8),
                                    nmask[:, t, :].rearrange("p (s r c) -> p s r c", r=ROWS, c=8), ALU.add).then_inc(S("nb"), 1)
                g.wait_ge(S("a_yt"), att_base("na", L) // HEADS + TILES - lo)
                g.dma_start(gn, bc(a["ret_gn"][L:L + 1, :])).then_inc(S("rtab"), 16)
                g.dma_start(rtab.rearrange("p a b -> p (a b)"), a["c_ret"]).then_inc(S("rtab"), 16)
                g.wait_ge(S("rtab"), B("rtab", L) + 32)
                for i in range(TILES - lo):
                    g.wait_ge(S("c5e"), B("c5e", L) + i + 1)
                    g.tensor_tensor(gate[:, i + lo, :], gate[:, i + lo, :], gn, ALU.mult).then_inc(S("c5d"), 1)
                g.wait_ge(S("c5d"), B("c5d", L) + TILES - lo)
                for i in range(TILES - lo):
                    o = on[:, i % 3, :]
                    g.wait_ge(S("rm"), B("rm", L) + i + 1)
                    g.tensor_tensor(o, o, gate[:, i + lo, :], ALU.mult).then_inc(S("rg"), 1)
                    g.wait_ge(S("rg"), B("rg", L) + i + 1)
                    g.tensor_tensor(o[:, 0:GW], o[:, 0:GW], o[:, GW:2 * GW], ALU.add).then_inc(S("ry"), 1)
                def gathers(i, first):
                    g.wait_ge(S("istg"), B("istg", L) + (1 if first else i + 2))
                    g.sem_inc(S("asked"), 1)
                    for s in range(SLOTS):
                        if first and s == (PH - 1) * TOPK:
                            g.wait_ge(S("istg"), B("istg", L) + 2)
                            g.sem_inc(S("asked"), 1)
                        if s >= UVRING or not first:
                            used = s - UVRING if s >= UVRING else s + UVRING * (slot_uses(s) - 1) - SLOTS
                            g.wait_ge(S("em"), B("em", L) + SLOTS * i + used + 1)
                            g.sem_inc(S("asked"), 1)
                        g.indirect_dma_start(uvr[:, s % UVRING, :], None, a["uv"],
                                             bass.IndirectOffsetOnAxis(ap=istage[:, s:s + 1], axis=0)).then_inc(S(f"uv{s % UVRING}"), 16)

                gathers(0, True)
                with g.Fori(1, TILES - lo) as i:
                    gathers(i, False)


_KERNEL_OUT = "out_0_dram"


def laid_out(inputs):
    x = {k: np.asarray(v) for k, v in inputs.items()}
    L = LAYERS
    p = {}
    p["x"] = x["x"][0]
    p["ctx"] = x["ctx"][0]
    p["c"] = np.stack([x["c_ctx"], x["c"][0]]).reshape(2, KD, P).transpose(2, 1, 0)
    for name in ("ada_w", "ada_b", "norm_mix_g", "w_in", "mla_kv_norm_g", "mla_w_ukv", "swa_sink", "w_out", "norm_ffn_g", "peer_wq"):
        p[name] = x[name]
    q = np.arange(P)
    dr = np.arange(ROWS)[None, :] - (q // 8 % ROWS)[:, None] + ROWS - 1
    dc = np.clip(np.arange(NA_PITCH)[None, :] - 16 - (8 * (q // HD) + q % 8)[:, None] + 15, 0, 30)
    rpb = x["na_rpb"][:, :, dr[:, :, None], dc[:, None, :]]
    p["rpb"] = rpb.transpose(0, 2, 1, 3, 4).reshape(L, P, HEADS * ROWS * NA_PITCH)
    p["decay_rows"] = np.concatenate([x["ret_decay_f"], x["ret_decay_b"]], 1)
    both = np.stack([x["ret_decay_f"], x["ret_decay_b"]], 2).reshape(L, 2, 2, 2)
    p["decay_cols"] = np.repeat(both.transpose(0, 2, 1, 3), HD, axis=1).reshape(L, P, 4)
    p["ret_gn"] = np.concatenate([x["ret_gn_f"], x["ret_gn_b"]], 1)
    p["mix_beta"] = x["mix_beta"].reshape(L, KD, P).transpose(0, 2, 1)
    p["keys"] = np.stack([x["peer_k1"], x["peer_k2"]], 1).transpose(0, 1, 3, 2)
    p["uv"] = np.concatenate([x["peer_u"], x["peer_v"]], 2).reshape(L * EXPERTS, 2 * D)
    p["final_norm_g"] = x["final_norm_g"][None]
    p.update(constants())
    return {k: np.ascontiguousarray(v) for k, v in p.items()}


def program(nc, p):
    a = {k: nc.dram_tensor(f"in_{k}_dram", v.shape, mybir.dt.from_np(v.dtype), kind="ExternalInput").ap() for k, v in p.items()}
    out = nc.dram_tensor(_KERNEL_OUT, (NLAT, D), F32, kind="ExternalOutput").ap()
    build(nc, a, out)


def kernel(**inputs):
    import concourse.bacc as bacc
    from concourse.bass_utils import run_bass_kernel_spmd as run

    p = laid_out(inputs)
    nc = bacc.Bacc("TRN2", target_bir_lowering=False, num_devices=1)
    program(nc, p)
    r = run(nc, [{f"in_{k}_dram": v for k, v in p.items()}], core_ids=[0])
    return r.results[0][_KERNEL_OUT].reshape(1, NLAT, D)
```
